# Optimizing a Trainium2 kernel written in Bass

```python
import jax, jax.numpy as jnp
from jax import lax
import numpy as np

D_MODEL = 2048
BATCH = 1
SEQ = 256
DEPTH = 1

GRID_W = 64
CTX_LEN = 256
F_WIDTH = D_MODEL // 2
F_GROUPS = 4
F_GW = F_WIDTH // F_GROUPS
M_HEADS = 8
M_WIDTH = D_MODEL // 2
M_DV = M_WIDTH // M_HEADS
M_DK = M_DV // 2
QK_WIDTH = 2 * M_HEADS * M_DK
N_GATES = 4 * M_HEADS
PROJ_WIDTH = F_WIDTH + QK_WIDTH + M_WIDTH + M_WIDTH + N_GATES
MIX_WIDTH = F_WIDTH + M_WIDTH
CHUNK = 64
CONV_K = 3
N_KEYS = 128
N_EXPERTS = N_KEYS * N_KEYS
PEER_HEADS = 8
PEER_TOPK = 16
PEER_QDIM = 256
PEER_BLOCK = 128
N_MOD = 6
EPS = 1e-6

kernel_name = 'hybrid_fnet_mlstm_peer_dit'

def rmsnorm(x, g):
    xf = x.astype(jnp.float32)
    y = xf * lax.rsqrt(jnp.mean(xf * xf, axis=-1, keepdims=True) + EPS)
    return (y * g.astype(jnp.float32)).astype(x.dtype)

def modulate(h, shift, scale):
    return h * (1 + scale) + shift

def split_proj(p, b_gate):
    o1 = F_WIDTH
    o2 = o1 + QK_WIDTH
    o3 = o2 + M_WIDTH
    o4 = o3 + M_WIDTH
    return p[..., :o1], p[..., o1:o2], p[..., o2:o3], p[..., o3:o4], p[..., o4:] + b_gate

def fourier_mix(u, g):
    B_, T, _ = u.shape
    uf = u.astype(jnp.float32).reshape(B_, T, F_GROUPS, F_GW)
    y = jnp.fft.fft2(uf, axes=(1, 3), norm='ortho').real
    return rmsnorm(y, g.reshape(F_GROUPS, F_GW)).reshape(B_, T, F_WIDTH).astype(u.dtype)

def conv_latent(u, w, rows):
    B_ = u.shape[0]
    img = u.reshape(B_, rows, GRID_W, QK_WIDTH)
    y = lax.conv_general_dilated(img, w[:, :, None, :].astype(u.dtype), (1, 1), 'SAME',
                                 dimension_numbers=('NHWC', 'HWIO', 'NHWC'),
                                 feature_group_count=QK_WIDTH)
    return y.reshape(u.shape)

def conv_context(u, w):
    y = lax.conv_general_dilated(u, w[CONV_K // 2][:, None, :].astype(u.dtype), (1,), 'SAME',
                                 dimension_numbers=('NWC', 'WIO', 'NWC'),
                                 feature_group_count=QK_WIDTH)
    return y

def mlstm_chunkwise(q, k, v, ig, lf, state):
    B_, H_, T, dk = q.shape
    dv = v.shape[-1]
    nc = T // CHUNK
    q = q.reshape(B_, H_, nc, CHUNK, dk)
    k = k.reshape(B_, H_, nc, CHUNK, dk)
    v = v.reshape(B_, H_, nc, CHUNK, dv)
    ig = ig.reshape(B_, H_, nc, CHUNK)
    lf = lf.reshape(B_, H_, nc, CHUNK)
    b = jnp.cumsum(lf, axis=-1)
    b_end = b[..., -1]
    a = b_end[..., None] - b + ig
    m_loc = jnp.max(a, axis=-1)
    kw = k * jnp.exp(a - m_loc[..., None])[..., None]
    C_chunk = jnp.einsum('bhcsk,bhcsv->bhckv', kw, v)
    n_chunk = jnp.sum(kw, axis=3)

    def step(carry, inp):
        C, n, m = carry
        Cc, ncnk, mc, be = inp
        m_new = jnp.maximum(be + m, mc)
        f_old = jnp.exp(be + m - m_new)
        f_new = jnp.exp(mc - m_new)
        C_new = f_old[..., None, None] * C + f_new[..., None, None] * Cc
        n_new = f_old[..., None] * n + f_new[..., None] * ncnk
        return (C_new, n_new, m_new), (C, n, m)

    xs = (jnp.moveaxis(C_chunk, 2, 0), jnp.moveaxis(n_chunk, 2, 0),
          jnp.moveaxis(m_loc, 2, 0), jnp.moveaxis(b_end, 2, 0))
    final, (C_prev, n_prev, m_prev) = lax.scan(step, state, xs)
    C_prev = jnp.moveaxis(C_prev, 0, 2)
    n_prev = jnp.moveaxis(n_prev, 0, 2)
    m_prev = jnp.moveaxis(m_prev, 0, 2)

    tri = jnp.tril(jnp.ones((CHUNK, CHUNK), dtype=bool))
    D = jnp.where(tri, b[..., :, None] - b[..., None, :] + ig[..., None, :], -jnp.inf)
    g = b + m_prev[..., None]
    m_j = jnp.maximum(g, jnp.max(D, axis=-1))
    S = jnp.einsum('bhcjk,bhcsk->bhcjs', q, k) * jnp.exp(D - m_j[..., None])
    inter = jnp.exp(g - m_j)
    num = inter[..., None] * jnp.einsum('bhcjk,bhckv->bhcjv', q, C_prev) + jnp.einsum('bhcjs,bhcsv->bhcjv', S, v)
    den = inter * jnp.einsum('bhcjk,bhck->bhcj', q, n_prev) + jnp.sum(S, axis=-1)
    h = num / jnp.maximum(jnp.abs(den), jnp.exp(-m_j))[..., None]
    return h.reshape(B_, H_, T, dv), final

def mlstm_mix(qk, v, o, gates, g, states):
    B_, T, _ = qk.shape
    heads = lambda t, d: t.astype(jnp.float32).reshape(B_, T, M_HEADS, d).transpose(0, 2, 1, 3)
    q = heads(qk[..., :QK_WIDTH // 2], M_DK)
    k = heads(qk[..., QK_WIDTH // 2:], M_DK) * (M_DK ** -0.5)
    vh = heads(v, M_DV)
    gt = gates.astype(jnp.float32).reshape(B_, T, 4, M_HEADS).transpose(2, 0, 3, 1)
    h_f, st_f = mlstm_chunkwise(q, k, vh, gt[0], jax.nn.log_sigmoid(gt[1]), states[0])
    rev = lambda t: jnp.flip(t, axis=2)
    h_b, st_b = mlstm_chunkwise(rev(q), rev(k), rev(vh), rev(gt[2]),
                                rev(jax.nn.log_sigmoid(gt[3])), states[1])
    h = (h_f + rev(h_b)).transpose(0, 2, 1, 3)
    h = rmsnorm(h, g.reshape(M_HEADS, M_DV)).reshape(B_, T, M_WIDTH)
    y = h * jax.nn.sigmoid(o.astype(jnp.float32))
    return y.astype(v.dtype), (st_f, st_b)

def peer(h, w_query, sub_keys, expert_u, expert_v):
    shape = h.shape
    blocks = h.reshape(-1, PEER_BLOCK, D_MODEL)

    def block(xb):
        q = (xb @ w_query).reshape(PEER_BLOCK, PEER_HEADS, 2, PEER_QDIM // 2)
        s = jnp.einsum('thpd,hpnd->thpn', q, sub_keys)
        sv, si = lax.top_k(s, PEER_TOPK)
        cand = (sv[:, :, 0, :, None] + sv[:, :, 1, None, :]).reshape(PEER_BLOCK, PEER_HEADS, PEER_TOPK * PEER_TOPK)
        cidx = (si[:, :, 0, :, None] * N_KEYS + si[:, :, 1, None, :]).reshape(PEER_BLOCK, PEER_HEADS, PEER_TOPK * PEER_TOPK)
        top_s, pos = lax.top_k(cand, PEER_TOPK)
        idx = jnp.take_along_axis(cidx, pos, axis=-1)
        gate = jax.nn.softmax(top_s.astype(jnp.float32), axis=-1)
        act = jax.nn.gelu(jnp.einsum('thkd,td->thk', expert_u[idx], xb).astype(jnp.float32))
        return jnp.einsum('thk,thkd->td', (gate * act).astype(xb.dtype), expert_v[idx])

    return lax.map(block, blocks).reshape(shape)

def setup_inputs(seed: int = 0) -> dict:
    key = jax.random.key(seed)
    ks = jax.random.split(key, 20)
    nrm = lambda k, shape, s: jax.random.normal(k, shape, jnp.float32) * s
    L, D = DEPTH, D_MODEL
    f_bias = jnp.linspace(3.0, 6.0, M_HEADS, dtype=jnp.float32)
    i_bias = jnp.zeros((M_HEADS,), jnp.float32)
    gate_base = jnp.concatenate([i_bias, f_bias, i_bias, f_bias])
    return {
        'x': nrm(ks[0], (BATCH, SEQ, D), 1.0),
        'c': nrm(ks[1], (BATCH, D), 1.0),
        'ctx': nrm(ks[2], (BATCH, CTX_LEN, D), 1.0),
        'c_ctx': nrm(ks[3], (D,), 1.0),
        'w_mod': nrm(ks[4], (L, D, N_MOD * D), 0.5 * D ** -0.5),
        'b_mod': nrm(ks[5], (L, N_MOD * D), 0.02),
        'g_norm_mix': 1.0 + nrm(ks[6], (L, D), 0.02),
        'g_norm_ffn': 1.0 + nrm(ks[7], (L, D), 0.02),
        'w_in': nrm(ks[8], (L, D, PROJ_WIDTH), D ** -0.5),
        'b_gate': gate_base + nrm(ks[9], (L, N_GATES), 0.1),
        'conv_qk': nrm(ks[10], (L, CONV_K, CONV_K, QK_WIDTH), 1.0 / CONV_K),
        'g_fourier': 1.0 + nrm(ks[11], (L, F_WIDTH), 0.02),
        'g_mlstm': 1.0 + nrm(ks[12], (L, M_WIDTH), 0.02),
        'w_out': nrm(ks[13], (L, MIX_WIDTH, D), MIX_WIDTH ** -0.5),
        'w_query': nrm(ks[14], (L, D, PEER_HEADS * PEER_QDIM), D ** -0.5),
        'sub_keys': nrm(ks[15], (L, PEER_HEADS, 2, N_KEYS, PEER_QDIM // 2), (PEER_QDIM // 2) ** -0.5),
        'expert_u': nrm(ks[16], (L, N_EXPERTS, D), D ** -0.5),
        'expert_v': nrm(ks[17], (L, N_EXPERTS, D), 1.0),
        'g_final': 1.0 + nrm(ks[18], (D,), 0.02),
    }

def reference(x, c, ctx, c_ctx, w_mod, b_mod, g_norm_mix, g_norm_ffn, w_in, b_gate, conv_qk,
              g_fourier, g_mlstm, w_out, w_query, sub_keys, expert_u, expert_v, g_final):
    B_, T, _ = x.shape
    rows = T // GRID_W
    zero = (jnp.zeros((B_, M_HEADS, M_DK, M_DV), jnp.float32),
            jnp.zeros((B_, M_HEADS, M_DK), jnp.float32),
            jnp.zeros((B_, M_HEADS), jnp.float32))
    for l in range(DEPTH):
        last = l == DEPTH - 1
        mod = jax.nn.silu(c) @ w_mod[l] + b_mod[l]
        mod_c = jax.nn.silu(c_ctx) @ w_mod[l] + b_mod[l]
        sh1, sc1, ga1, sh2, sc2, ga2 = jnp.split(mod[:, None, :], N_MOD, axis=-1)
        csh1, csc1, cga1, csh2, csc2, cga2 = jnp.split(mod_c, N_MOD)

        pc = modulate(rmsnorm(ctx, g_norm_mix[l]), csh1, csc1) @ w_in[l]
        four_c, qk_c, v_c, o_c, gates_c = split_proj(pc, b_gate[l])
        qk_c = jax.nn.silu(conv_context(qk_c, conv_qk[l]))
        y_mc, ctx_states = mlstm_mix(qk_c, v_c, o_c, gates_c, g_mlstm[l], (zero, zero))

        p = modulate(rmsnorm(x, g_norm_mix[l]), sh1, sc1) @ w_in[l]
        four, qk, v, o, gates = split_proj(p, b_gate[l])
        qk = jax.nn.silu(conv_latent(qk, conv_qk[l], rows))
        y_m, _ = mlstm_mix(qk, v, o, gates, g_mlstm[l], ctx_states)
        y = jnp.concatenate([fourier_mix(four, g_fourier[l]), y_m], axis=-1) @ w_out[l]
        x = x + ga1 * y
        h2 = modulate(rmsnorm(x, g_norm_ffn[l]), sh2, sc2)
        x = x + ga2 * peer(h2, w_query[l], sub_keys[l], expert_u[l], expert_v[l])

        if not last:
            yc = jnp.concatenate([fourier_mix(four_c, g_fourier[l]), y_mc], axis=-1) @ w_out[l]
            ctx = ctx + cga1 * yc
            hc2 = modulate(rmsnorm(ctx, g_norm_ffn[l]), csh2, csc2)
            ctx = ctx + cga2 * peer(hc2, w_query[l], sub_keys[l], expert_u[l], expert_v[l])
    return rmsnorm(x, g_final)


_drawn_inputs = setup_inputs


def setup_inputs(seed=0):
    import zlib

    import numpy as np

    out = dict(_drawn_inputs(seed))
    spreads = {}
    factors = {'g_norm_mix': 3.939,
     'g_fourier': 46.945,
     'g_mlstm': 74.277,
     'g_final': 23.292,
     'g_norm_ffn': 12.7}
    for name, (base, spread) in spreads.items():
        noise = np.random.default_rng([zlib.crc32(name.encode()), seed]).standard_normal(out[name].shape)
        drawn = base * np.exp(spread * noise) if base else spread * noise
        out[name] = __import__('jax').numpy.asarray(drawn.astype(out[name].dtype))
    for name, factor in factors.items():
        out[name] = (out[name] * factor).astype(out[name].dtype)
    return out
```

```python
from contextlib import ExitStack

import numpy as np

import concourse.bass as bass
from concourse import mybir
from concourse.alu_op_type import AluOpType as ALU

F32 = mybir.dt.float32
U32 = mybir.dt.uint32
ACT = mybir.ActivationFunctionType
AX_X = mybir.AxisListType.X

P = 128
D = 2048
KB = D // P
T = 256
TB = T // P
GRID_W = 64
ROWS = T // GRID_W
CH = 512
KH = KB // 2
FW = D // 2
FG = 4
GW = FW // FG
MH = 8
DV = 128
DK = 64
EPS = 1e-6
PH = 8
NK = 128
TOPK = 16
FAR = -1e30
LOWEST = -3e38

C_ID = 0
C_DFT = C_ID + P
C_MASK = C_DFT + 2 * CH
C_IOTA = C_MASK + 2 * P
C_ONE = C_IOTA + 16
C_EPS = C_ONE + 32
C_ZERO = C_EPS + 1
C_ALL = C_ZERO + P + 15

V_C = 0
V_B = 32
V_G = 64
V_CONV = 80
V_ALL = V_CONV + 72

W_IN_CHUNKS = [3, 2, 4, 5, 0, 1, 6, 7]
GATE_ROWS = [0, 64, 32, 96]
NG = 104
MODB = 16


def constants():
    c = np.zeros((P, C_ALL), np.float32)
    c[:, C_ID:C_ID + P] = np.eye(P)
    for b in range(2):
        a = 2 * np.pi * ((np.outer(b * P + np.arange(P), np.arange(T))) % T) / T
        c[:, C_DFT + b * CH:C_DFT + b * CH + T] = np.cos(a)
        c[:, C_DFT + b * CH + T:C_DFT + (b + 1) * CH] = np.sin(a)
    s, j = np.meshgrid(np.arange(P), np.arange(P), indexing="ij")
    c[:, C_MASK:C_MASK + P] = np.where(s <= j, 0.0, FAR)
    c[:, C_MASK + P:C_MASK + 2 * P] = np.where(s >= j, 0.0, FAR)
    c[:, C_IOTA:C_IOTA + 16] = np.arange(16)
    c[:, C_ONE:C_ONE + 32] = 1.0
    c[:, C_EPS] = EPS
    return c


def build(nc, x, c, ctx, c_ctx, w_mod, b_mod, g_norm_mix, g_norm_ffn, w_in, b_gate, conv_qk,
          g_fourier, g_mlstm, w_out, w_query, sub_keys, expert_u, expert_v, g_final, consts, out):
    with ExitStack() as stack:
        def sb(name, shape, dt=F32):
            return stack.enter_context(nc.sbuf_tensor(name, shape, dt))

        def sem(name):
            return stack.enter_context(nc.semaphore(name))

        ps = stack.enter_context(nc.psum_tensor("ps", [P, 8, CH], F32))
        ring = sb("ring", [P, 8, D])
        A = sb("A", [P, TB, D])
        B = sb("B", [P, TB, D])
        H = sb("H", [P, KB, CH])
        KT = sb("KT", [P, 4, 2 * T])
        QT = sb("QT", [P, 4, T])
        VX = sb("VX", [P, 4, MH, DV + 1])
        modrow = sb("modrow", [P, D])
        gy = sb("gy", [P, D])
        K = sb("K", [P, C_ALL])
        wg = sb("wg", [P, KB, NG])
        acc = sb("acc", [P, 2, CH])
        rows = sb("rows", [32, 3 * P])
        vec = sb("vec", [P, V_ALL])
        shT = sb("shT", [P, 2, KB])
        gT = sb("gT", [P, 2, KB])
        gsb = sb("gsb", [NG, 2 * T])
        t1 = sb("t1", [40, 2 * T])
        t2 = sb("t2", [40, 2 * T])
        negm = sb("negm", [40, T])
        bg = sb("bg", [NG, 1])
        uT = sb("uT", [P, 6, 40])
        st = sb("st", [P, 64])
        small = sb("small", [P, 16])

        ident = K[:, C_ID:C_ID + P]
        ones32 = K[:, C_ONE:C_ONE + 32]
        eps = K[:, C_EPS:C_EPS + 1]
        zeros = K[:, C_ZERO:C_ZERO + P]
        dft = K[:, C_DFT:C_DFT + 2 * CH].rearrange("p (b n) -> p b n", b=2)
        flat = lambda t: t[:].rearrange("p a b -> p (a b)")
        ringf, Hf, KTf, QTf = flat(ring), flat(H), flat(KT), flat(QT)
        VXf = VX[:].rearrange("p a b c -> p (a b c)")
        W = [ringf[:, i * KH * CH:(i + 1) * KH * CH].rearrange("p (k n) -> p k n", k=KH)
             for i in range(4)]
        moda = VXf[0:2, 0:2 * D]
        conv_rows = QTf[0:9, 0:2 * CH]
        kraw = B[:, 0, :].rearrange("p (j t) -> p j t", j=4)
        qraw = B[:, 1, 0:4 * T].rearrange("p (j t) -> p j t", j=4)
        wexp = Hf[:, 0:4096].rearrange("p (r d s j) -> p r d s j", r=2, d=2, s=4)
        hm = Hf[:, 4096:6144].rearrange("p (b n) -> p b n", b=2)
        pts = Hf[:, 6144:8192].rearrange("p (r b n) -> p r b n", r=2, b=2)
        tmp = ringf[:, 0:4 * D]
        yT = Hf[:, 0:4096].rearrange("p (k t) -> p k t", k=KB)
        ga1, sh2 = Hf[:, 4096:6144], Hf[:, 6144:8192]
        ga2 = KTf[:, 0:D]
        g2 = VXf[:, 0:D]
        h2T = yT
        qhT = Hf[:, 4096:8192].rearrange("p (k t) -> p k t", k=KB)
        keys_raw = gy[:].rearrange("p (h n) -> p h n", h=2 * PH)
        keysT = modrow[:].rearrange("p (h n) -> p h n", h=2 * PH)
        sc = ringf[:, 4 * D:6 * D].rearrange("p (b h n) -> p b h n", b=TB, h=2 * PH)
        cand = ring[:, 6, :]
        work = ring[:, 7, :]
        pe0 = D
        sv = VXf[:, pe0:pe0 + 256]
        si = VXf[:, pe0 + 256:pe0 + 512]
        top = VXf[:, pe0 + 512:pe0 + 640]
        sel = VXf[:, pe0 + 640:pe0 + 896]
        gate = VXf[:, pe0 + 896:pe0 + 1152]
        dots = VXf[:, pe0 + 1152:pe0 + 1408]
        wgt = VXf[:, pe0 + 1408:pe0 + 1664]
        act_t = VXf[:, pe0 + 1664:pe0 + 1920]
        siu = QTf[:, 0:256].bitcast(U32)
        pos = QTf[:, 256:384].bitcast(U32)
        half = QTf[:, 384:512].bitcast(U32)
        halff = QTf[:, 512:640]
        eidx = acc[:].rearrange("p a b -> p (a b)")[:, 0:256].bitcast(U32)
        eflt = acc[:].rearrange("p a b -> p (a b)")[:, 256:384]
        sums = acc[:].rearrange("p a b -> p (a b)")[:, 384:400]
        diag = wg[:].rearrange("p a b -> p (a b)")[:, 0:4 * P].rearrange("p (s n) -> p s n", s=4)
        slot_idx = wg[:].rearrange("p a b -> p (a b)")[:, 4 * P:4 * P + 8].bitcast(U32)

        names = """ld_const ld_c ld_rows ld_x ld_ctx ld_wg ld_bg ld_gy ld_bm ld_x2 ld_gffn ld_keys ld_gfin
        wg_zero modrow_zero silu_c vec_psum vec_ready moda_free modcol_psum mod_ready ssq std
        rstd xn_ready xT_psum ht_act ht_dve w_free m_free modb_red modb_free proj_free
        gates_psum abs_ready ln_ready thr_in thr_ready u_ready uT_psum uT_ready kconv qconv
        k_ready q_ready ones_v fn1_done fn1_free fn2_done fn2_free s_done diag_in exp_done
        p_done num_done num_free y_ready yT_psum yT_ready bc_psum bc_free g2_ready o_sig hsq out_free
        x1_ready ssq2 std2 h2_ready h2T_psum h2T_ready keys_psum keys_ready q_free score_psum
        score_ready top_in gate_e peer_in u_free pair_free dots_ready gelu_done wgt_ready
        diag_ready copied ssq3 std3 final_ready stored dve act""".split()
        S = {n: sem(n) for n in names}
        w_ld = [sem(f"w_ld{i}") for i in range(2)]
        m_ld = [sem(f"m_ld{i}") for i in range(2)]
        u_ld = [sem(f"u_ld{i}") for i in range(4)]
        v_ld = [sem(f"v_ld{i}") for i in range(4)]

        def chain(engine, name):
            count = [0]

            def link(ins):
                count[0] += 1
                ins.then_inc(S[name], 1)
                engine.wait_ge(S[name], count[0])
            return link

        block = stack.enter_context(nc.Block())

        @block.sync
        def _(sp):
            sp.dma_start(K[:], consts).then_inc(S["ld_const"], 16)

            def load(piece, src, kh, n0):
                sp.dma_start(W[piece % 2], src[kh * KH * P:(kh + 1) * KH * P, n0].rearrange(
                    "(k p) n -> p k n", p=P)).then_inc(w_ld[piece % 2], 16)

            wm, wi = w_mod[0], w_in[0]
            for kh in range(2):
                load(kh, wm, kh, bass.ds(0, CH))
            sp.dma_start(A[:], x[0].rearrange("(b p) d -> p b d", p=P)).then_inc(S["ld_x"], 16)
            sp.dma_start(B[:], ctx[0].rearrange("(b p) d -> p b d", p=P)).then_inc(S["ld_ctx"], 16)
            with sp.Fori(1, 8) as n:
                for kh in range(2):
                    sp.wait_ge(S["w_free"], n * 2 + (kh - 1))
                    load(kh, wm, kh, bass.ds(n * CH, CH))
            for i, n in enumerate(W_IN_CHUNKS):
                for kh in range(2):
                    sp.wait_ge(S["w_free"], 16 + 2 * i + kh - 1)
                    load(kh, wi, kh, bass.ds(n * CH, CH))
            sp.wait_ge(S["y_ready"], 1)
            for base, src in ((32, w_out[0]), (40, w_query[0])):
                with sp.Fori(0, 4) as n:
                    for kh in range(2):
                        sp.wait_ge(S["w_free"], n * 2 + (base + kh - 1))
                        load(kh, src, kh, bass.ds(n * CH, CH))
            sp.wait_ge(S["final_ready"], 1)
            sp.dma_start(out[0].rearrange("(b p) d -> p b d", p=P), B[:]).then_inc(S["stored"], 16)
            sp.wait_ge(S["stored"], 16)

        @block.gpsimd
        def _(pool):
            nc.gpsimd.memset(wg[:], 0.0).then_inc(S["wg_zero"], 1)
            nc.gpsimd.memset(bg[:], 0.0).then_inc(S["wg_zero"], 1)
            nc.gpsimd.memset(modrow[:], 0.0).then_inc(S["modrow_zero"], 1)
            pool.wait_ge(S["wg_zero"], 2)
            gates0 = 8 * CH
            for g, r in enumerate(GATE_ROWS):
                pool.dma_start(wg[:, :, r:r + MH],
                               w_in[0][:, gates0 + g * MH:gates0 + (g + 1) * MH].rearrange(
                                   "(k p) n -> p k n", p=P)).then_inc(S["ld_wg"], 16)
                pool.dma_start(bg[r:r + MH, :], b_gate[0:1, g * MH:(g + 1) * MH].rearrange(
                    "a n -> n a")).then_inc(S["ld_bg"], 16)
            pool.wait_ge(S["modrow_zero"], 1)
            for r in range(4):
                pool.dma_start(modrow[32 * r:32 * r + 1, :], b_mod[0:1, (2 + r) * D:(3 + r) * D]
                               ).then_inc(S["ld_bm"], 16)
            pool.dma_start(gy[:, 0:FW], g_fourier.to_broadcast([P, FW])).then_inc(S["ld_gy"], 16)
            pool.dma_start(gy[:, FW:D], g_mlstm.to_broadcast([P, FW])).then_inc(S["ld_gy"], 16)

            pool.wait_ge(S["w_free"], 13)
            wm = w_mod[0]

            def load(m, kh):
                pool.dma_start(W[2 + kh], wm[kh * KH * P:(kh + 1) * KH * P,
                                             bass.ds(m * CH + 2 * D, CH)].rearrange(
                    "(k p) n -> p k n", p=P)).then_inc(m_ld[kh], 16)
            for kh in range(2):
                load(0, kh)
            with pool.Fori(1, MODB) as m:
                for kh in range(2):
                    pool.wait_ge(S["m_free"], m * 2 + (kh - 1))
                    load(m, kh)
            pool.wait_ge(S["kconv"], 4)
            pool.wait_ge(S["qconv"], 4)
            pool.dma_start(B[:], x[0].rearrange("(b p) d -> p b d", p=P)).then_inc(S["ld_x2"], 16)
            pool.wait_ge(S["num_done"], 4 * MH)
            pool.dma_start(g2, g_norm_ffn.to_broadcast([P, D])).then_inc(S["ld_gffn"], 16)
            pool.wait_ge(S["y_ready"], 1)
            pool.dma_start(keys_raw, sub_keys[0].rearrange("h p n d -> n (h p) d")
                           ).then_inc(S["ld_keys"], 16)
            pool.wait_ge(S["keys_psum"], 16)
            pool.dma_start(gy[:], g_final.rearrange("(a d) -> a d", a=1).to_broadcast([P, D])
                           ).then_inc(S["ld_gfin"], 16)

            def gather(table, slot, rank, index, count, loaded):
                nc.gpsimd.tensor_copy(index, eidx[:, bass.ds(rank, 1)]).then_inc(S["copied"], 1)
                pool.wait_ge(S["copied"], count)
                pool.nop(nofuse=True)
                nc.gpsimd.indirect_dma_start(
                    ring[:, slot, :], None, table, bass.IndirectOffsetOnAxis(ap=index, axis=0)
                ).then_inc(loaded, 16)

            def gather_u(q, s, count):
                pool.wait_ge(S["u_free"], q * 4 + (s + 1))
                gather(expert_u[0], s, q * 4 + s, slot_idx[:, s:s + 1], count, u_ld[s])

            def gather_v(q, s, count):
                pool.wait_ge(S["pair_free"], q * 4 + (s + 1))
                gather(expert_v[0], 4 + s, q * 4 + s, slot_idx[:, 4 + s:5 + s], count, v_ld[s])

            pool.wait_ge(S["peer_in"], 1)
            lag = 4
            last = TB * PH * TOPK // 4
            with pool.Fori(0, lag) as q:
                for s in range(4):
                    gather_u(q, s, q * 4 + (s + 1))
            with pool.Fori(lag, last) as q:
                for s in range(4):
                    gather_u(q, s, q * 8 + (2 * s + 1 - 4 * lag))
                    gather_v(q - lag, s, q * 8 + (2 * s + 2 - 4 * lag))
            with pool.Fori(last, last + lag) as q:
                for s in range(4):
                    gather_v(q - lag, s, q * 4 + (s + 1 + 4 * (last - lag)))

        @block.scalar
        def _(act):
            link = chain(act, "act")
            nc_a = nc.scalar
            act.dma_start(rows[0:KB, 0:P], c[0].rearrange("(k p) -> k p", p=P)).then_inc(S["ld_c"], 16)
            act.dma_start(rows[KB:2 * KB, 0:P], c_ctx.rearrange("(k p) -> k p", p=P)
                          ).then_inc(S["ld_c"], 16)
            act.dma_start(rows[0:32, P:2 * P], b_mod[0, 0:2 * D].rearrange("(k p) -> k p", p=P)
                          ).then_inc(S["ld_rows"], 16)
            act.dma_start(rows[0:KB, 2 * P:3 * P], g_norm_mix[0].rearrange("(k p) -> k p", p=P)
                          ).then_inc(S["ld_rows"], 16)
            act.dma_start(conv_rows, conv_qk[0].rearrange("a b n -> (a b) n")
                          ).then_inc(S["ld_rows"], 16)
            act.wait_ge(S["ld_c"], 32)
            nc_a.activation(rows[:, 0:P], rows[:, 0:P], ACT.Silu).then_inc(S["silu_c"], 1)

            act.wait_ge(S["ld_const"], 16)
            for i, (tile, loaded) in enumerate(((B, "ld_ctx"), (A, "ld_x"))):
                act.wait_ge(S[loaded], 16)
                for b in range(TB):
                    o = (2 * i + b) * D
                    nc_a.activation(Hf[:, o:o + D], tile[:, b, :], ACT.Square,
                                    accum_out=st[:, 2 * i + b:2 * i + b + 1]).then_inc(S["ssq"], 1)
            act.wait_ge(S["ssq"], 4)
            nc_a.activation(st[:, 4:8], st[:, 0:4], ACT.Sqrt, bias=eps, scale=1.0 / D
                            ).then_inc(S["std"], 1)

            act.wait_ge(S["mod_ready"], 1)
            for k in range(0, KB, 2):
                act.wait_ge(S["xT_psum"], k + 1)
                for side, c_ in ((0, 1), (1, 0)):
                    cols = slice(side * T, (side + 1) * T)
                    ins = nc_a.activation(H[:, k, cols], ps[:, k % 6, cols], ACT.Identity,
                                          bias=shT[:, c_, k:k + 1], scale=gT[:, c_, k:k + 1])
                ins.then_inc(S["ht_act"], 1)

            act.wait_ge(S["ld_bg"], 64)
            act.wait_ge(S["gates_psum"], 1)
            nc_a.activation(gsb[:], ps[0:NG, 0, :], ACT.Identity, bias=bg[:]
                            ).then_inc(S["proj_free"], 1)
            group = 1
            for i, n in enumerate(W_IN_CHUNKS):
                wide = i < 4
                act.wait_ge(S["w_free"], 16 + 2 * (i + 1))
                for j in range(4 if wide else 2):
                    bank = ps[:, group % 7, :]
                    if n == 3:
                        dst, src = kraw[:, j, :], bank
                    elif n == 2:
                        dst, src = qraw[:, j, :], bank[:, 0:T]
                    elif wide:
                        h0 = (n - 4) * 4
                        dst = VX[:, j, h0:h0 + 4, 0:DV]
                        src = bank.rearrange("p (h d) -> p h d", h=4)
                    else:
                        col = n * CH if n < 2 else FW + (n - 6) * CH
                        dst, src = A[:, j, col:col + CH], bank
                    nc_a.copy(dst, src).then_inc(S["proj_free"], 1)
                    group += 1
            for b in range(4):
                ins = nc_a.activation(VX[:, b, :, DV:DV + 1], K[:, C_ONE:C_ONE + MH].unsqueeze(2),
                                      ACT.Copy)
            ins.then_inc(S["ones_v"], 1)

            for j in range(4):
                act.wait_ge(S["kconv"], j + 1)
                nc_a.activation(KT[:, j, :], KT[:, j, :], ACT.Silu).then_inc(S["k_ready"], 1)
            for j in range(4):
                act.wait_ge(S["qconv"], j + 1)
                nc_a.activation(QT[:, j, :], QT[:, j, :], ACT.Silu).then_inc(S["q_ready"], 1)
            act.wait_ge(S["proj_free"], 25)
            nc_a.activation(A[:, :, FW:D], A[:, :, FW:D], ACT.Sigmoid).then_inc(S["o_sig"], 1)

            act.wait_ge(S["abs_ready"], 1)
            link(nc_a.activation(t2[:], t2[:], ACT.Exp, scale=-1.0))
            nc_a.activation(t2[:], t2[:], ACT.Ln, bias=K[0:40, C_ONE:C_ONE + 1]
                            ).then_inc(S["ln_ready"], 1)
            act.wait_ge(S["thr_in"], 1)
            nc_a.activation(t2[:, T:2 * T], t2[:, T:2 * T], ACT.Exp, scale=-1.0
                            ).then_inc(S["thr_ready"], 1)

            for g in range(FG):
                act.wait_ge(S["fn1_done"], g + 1)
                if g >= 2:
                    act.wait_ge(S["fn2_done"], g - 1)
                for b in range(2):
                    src = ps[:, 2 * (g % 2) + b, :]
                    nc_a.mul(pts[:, g % 2, b, 0:T], src[:, 0:T], 1.0 / T)
                    nc_a.mul(pts[:, g % 2, b, T:2 * T], src[:, T:2 * T], -1.0 / T
                             ).then_inc(S["fn1_free"], 1)
            for g in range(FG):
                act.wait_ge(S["fn2_done"], g + 1)
                for b in range(TB):
                    src = ps[:, 4 + g % 4, b * T:(b + 1) * T]
                    nc_a.copy(A[:, b, g * GW:(g + 1) * GW], src)
                    nc_a.activation(tmp[:, (g * 2 + b) * GW:(g * 2 + b + 1) * GW], src, ACT.Square,
                                    accum_out=st[:, 8 + b * FG + g:9 + b * FG + g]
                                    ).then_inc(S["fn2_free"], 1)

            act.wait_ge(S["uT_ready"], 1)
            for h in range(MH):
                act.wait_ge(S["diag_in"], 2 * (h + 1))
                if h >= 2:
                    act.wait_ge(S["num_done"], 4 * (h - 1))
                for d in range(2):
                    r = 32 * d + h
                    w = wexp[:, h % 2, d]
                    mb = ps[:, 4 + h % 2, d * T:(d + 1) * T]
                    for b in range(2):
                        nc_a.activation(w[:, b, :], mb, ACT.Exp, bias=uT[:, b, r:r + 1])
                    off, cols = (2, slice(P, T)) if d == 0 else (3, slice(0, P))
                    nc_a.activation(w[:, off, cols], mb[:, cols], ACT.Exp,
                                    bias=uT[:, off, r:r + 1])
                    for b in range(2):
                        ins = nc_a.activation(w[:, 2 + b, b * P:(b + 1) * P],
                                              w[:, 2 + b, b * P:(b + 1) * P], ACT.Exp)
                    ins.then_inc(S["exp_done"], 1)

            act.wait_ge(S["hsq"], 1)
            nc_a.activation(st[:, 32:40], st[:, 8:16], ACT.Sqrt, bias=eps, scale=1.0 / GW)
            nc_a.activation(st[:, 40:56], st[:, 16:32], ACT.Sqrt, bias=eps, scale=1.0 / DV
                            ).then_inc(S["std"], 1)

            for k in range(KB):
                act.wait_ge(S["yT_psum"], k + 1)
                nc_a.copy(yT[:, k, :], ps[:, k % 4, 0:T]).then_inc(S["yT_ready"], 1)
            for i, dst in enumerate((ga1, sh2, ga2)):
                for n in range(4):
                    act.wait_ge(S["bc_psum"], 4 * i + n + 1)
                    nc_a.copy(dst[:, n * CH:(n + 1) * CH], ps[:, 4 + n, :]).then_inc(S["bc_free"], 1)

            act.wait_ge(S["x1_ready"], 8)
            for b in range(TB):
                nc_a.activation(A[:, b, :], B[:, b, :], ACT.Square, accum_out=st[:, b:b + 1]
                                ).then_inc(S["ssq2"], 1)
            act.wait_ge(S["ssq2"], 2)
            nc_a.activation(st[:, 2:4], st[:, 0:2], ACT.Sqrt, bias=eps, scale=1.0 / D
                            ).then_inc(S["std2"], 1)
            for i in range(4):
                act.wait_ge(S["keys_psum"], 4 * (i + 1))
                nc_a.copy(keysT[:, 4 * i:4 * i + 4, :],
                          ps[:, i, :].rearrange("p (h n) -> p h n", h=4)).then_inc(S["keys_ready"], 1)
            for k in range(KB):
                act.wait_ge(S["h2T_psum"], k + 1)
                nc_a.copy(h2T[:, k, :], ps[:, 4 + k % 4, 0:T]).then_inc(S["h2T_ready"], 1)
            for k in range(KB):
                if k % 4 == 0:
                    act.wait_ge(S["w_free"], 40 + 2 * (k // 4 + 1))
                nc_a.copy(qhT[:, k, :], ps[:, k % 8, 0:T]).then_inc(S["q_free"], 1)
            for b in range(TB):
                for i in range(4):
                    act.wait_ge(S["score_psum"], 4 * b + i + 1)
                    nc_a.copy(sc[:, b, 4 * i:4 * i + 4, :],
                              ps[:, 4 * b + i, :].rearrange("p (h n) -> p h n", h=4)
                              ).then_inc(S["score_ready"], 1)
            for b in range(TB):
                act.wait_ge(S["top_in"], b + 1)
                nc_a.activation(gate[:, b * P:(b + 1) * P], gate[:, b * P:(b + 1) * P], ACT.Exp
                                ).then_inc(S["gate_e"], 1)

            with act.Fori(0, TB * PH) as g:
                act.wait_ge(S["dots_ready"], g + 1)
                nc_a.activation(act_t[:, bass.ds(g * TOPK, TOPK)], dots[:, bass.ds(g * TOPK, TOPK)],
                                ACT.Gelu_apprx_tanh).then_inc(S["gelu_done"], 1)
                act.wait_ge(S["wgt_ready"], g + 1)
                for r in range(TOPK):
                    act.wait_ge(S["pair_free"], g * TOPK + (r + 1))
                    nc_a.activation(diag[:, r % 4, :], ident, ACT.Copy,
                                    scale=wgt[:, bass.ds(g * TOPK + r, 1)]
                                    ).then_inc(S["diag_ready"], 1)
            for b in range(TB):
                act.wait_ge(S["ssq3"], b + 1)
                nc_a.activation(A[:, b, :], B[:, b, :], ACT.Square, accum_out=st[:, b:b + 1]
                                ).then_inc(S["act"], 1)
            act.wait_ge(S["act"], 1 + TB)
            nc_a.activation(st[:, 2:4], st[:, 0:2], ACT.Sqrt, bias=eps, scale=1.0 / D
                            ).then_inc(S["std3"], 1)

        @block.tensor
        def _(pe):
            mm, tr = nc.tensor.matmul, nc.tensor.transpose
            pe.wait_ge(S["ld_const"], 16)
            pe.wait_ge(S["silu_c"], 1)
            pe.wait_ge(S["ld_rows"], 48)
            tr(ps[:, 7, V_C:V_C + 32], rows[:, 0:P], ident[0:32, 0:32])
            tr(ps[:, 7, V_B:V_B + 32], rows[:, P:2 * P], ident[0:32, 0:32])
            tr(ps[:, 7, V_G:V_G + KB], rows[0:KB, 2 * P:3 * P], ident[0:KB, 0:KB])
            for j in range(8):
                ins = tr(ps[:, 7, V_CONV + 9 * j:V_CONV + 9 * j + 9],
                         conv_rows[:, j * P:(j + 1) * P], ident[0:9, 0:9])
            ins.then_inc(S["vec_psum"], 1)

            pe.wait_ge(S["vec_ready"], 1)
            with pe.Fori(0, 4) as n2:
                for par in range(2):
                    pe.wait_ge(S["moda_free"], n2 * 2 + (par + 1))
                    for kh in range(2):
                        pe.wait_ge(w_ld[kh], n2 * 32 + (16 * par + 16))
                        for k in range(KH):
                            kk = kh * KH + k
                            ins = mm(ps[0:2, par, :], vec[:, kk:32:KB], W[kh][:, k, :],
                                     start=kk == 0, stop=kk == KB - 1)
                        ins.then_inc(S["w_free"], 1)
            pe.wait_ge(S["moda_free"], 2 + 8)
            for j in range(2 * KB):
                ins = tr(ps[:, 7, 2 * j:2 * j + 2], moda[:, j * P:(j + 1) * P], ident[0:2, 0:2])
            ins.then_inc(S["modcol_psum"], 1)

            pe.wait_ge(S["xn_ready"], 4)
            for k in range(KB):
                if k >= 6:
                    pe.wait_ge(S[("ht_act", "ht_dve")[k % 2]], k // 2 - 2)
                for b in range(4):
                    src = (B, A)[b // 2][:, b % 2, k * P:(k + 1) * P]
                    ins = tr(ps[:, k % 6, b * P:(b + 1) * P], src, ident)
                ins.then_inc(S["xT_psum"], 1)
            pe.wait_ge(S["ht_act"], KB // 2)
            pe.wait_ge(S["ht_dve"], KB // 2)

            pe.wait_ge(S["ld_wg"], 64)
            for k in range(KB):
                ins = mm(ps[0:NG, 0, :], wg[:, k, :], H[:, k, :], start=k == 0, stop=k == KB - 1)
            ins.then_inc(S["gates_psum"], 1)

            def reduce_modb(m):
                pe.wait_ge(S["m_free"], 2 * (m + 1))
                if m >= 1:
                    pe.wait_ge(S["modb_free"], m)
                r = 32 * (m // 4)
                mm(ps[r:r + 32, 7, :], ones32, acc[:, m % 2, :], start=True, stop=True
                   ).then_inc(S["modb_red"], 1)

            group = 1
            for i, n in enumerate(W_IN_CHUNKS):
                count = 4 if i < 4 else 2
                for kh in range(2):
                    piece = 2 * i + kh
                    pe.wait_ge(w_ld[kh], 16 * (8 + i + 1))
                    for j in range(count):
                        if kh == 0 and group + j >= 7:
                            pe.wait_ge(S["proj_free"], group + j - 6)
                        bank = ps[:, (group + j) % 7, :]
                        for k in range(KH):
                            kk = kh * KH + k
                            flags = dict(start=kk == 0, stop=kk == KB - 1)
                            if n == 3:
                                ins = mm(bank, W[kh][:, k, j * P:(j + 1) * P], H[:, kk, :], **flags)
                            elif n == 2:
                                ins = mm(bank[:, 0:T], W[kh][:, k, j * P:(j + 1) * P],
                                         H[:, kk, T:2 * T], **flags)
                            else:
                                b = j if count == 4 else 2 + j
                                ins = mm(bank, H[:, kk, b * P:(b + 1) * P], W[kh][:, k, :], **flags)
                    ins.then_inc(S["w_free"], 1)
                    if piece >= 1:
                        reduce_modb(piece - 1)
                group += count
            reduce_modb(MODB - 1)

            pe.wait_ge(S["proj_free"], 25)
            pe.wait_ge(S["modb_free"], MODB)

            def positions(g):
                if g >= 2:
                    pe.wait_ge(S["fn1_free"], 2 * (g - 1))
                for b in range(2):
                    for t in range(TB):
                        ins = mm(ps[:, 2 * (g % 2) + b, :],
                                 A[:, t, g * GW + b * P:g * GW + (b + 1) * P], dft[:, t, :],
                                 start=t == 0, stop=t == TB - 1)
                ins.then_inc(S["fn1_done"], 1)

            def channels(g):
                pe.wait_ge(S["fn1_free"], 2 * (g + 1))
                for t in range(TB):
                    for i in range(4):
                        part, b = i // 2, i % 2
                        ins = mm(ps[:, 4 + g % 4, t * T:(t + 1) * T],
                                 pts[:, g % 2, b, part * T + t * P:part * T + (t + 1) * P],
                                 dft[:, b, part * T:(part + 1) * T], start=i == 0, stop=i == 3)
                ins.then_inc(S["fn2_done"], 1)

            positions(0)
            for g in range(FG):
                if g + 1 < FG:
                    positions(g + 1)
                channels(g)

            pe.wait_ge(S["fn2_free"], 2 * FG)
            pe.wait_ge(S["u_ready"], 1)
            pe.wait_ge(S["thr_ready"], 1)
            for b in range(4):
                tr(ps[:, 6, b * 40:(b + 1) * 40], gsb[0:40, b * P:(b + 1) * P], ident[0:40, 0:40])
            for b in range(2):
                ins = tr(ps[:, 6, (4 + b) * 40:(5 + b) * 40], t2[:, T + b * P:T + (b + 1) * P],
                         ident[0:40, 0:40])
            ins.then_inc(S["uT_psum"], 1)
            pe.wait_ge(S["k_ready"], 4)
            pe.wait_ge(S["q_ready"], 4)
            pe.wait_ge(S["ones_v"], 1)
            pe.wait_ge(S["uT_ready"], 1)

            def scores(h):
                if h >= 2:
                    pe.wait_ge(S["p_done"], 2 * (h - 1))
                    pe.wait_ge(S["exp_done"], 2 * (h - 1))
                r0 = (h % 2) * DK
                q = QT[r0:r0 + DK, h // 2, :]
                for b in range(4):
                    mm(ps[:, 2 * (h % 2) + b // 2, (b % 2) * T:(b % 2 + 1) * T],
                       KT[r0:r0 + DK, h // 2, b * P:(b + 1) * P], q, start=True, stop=True)
                for d in range(2):
                    r = 32 * d + h
                    ins = mm(ps[:, 4 + h % 2, d * T:(d + 1) * T],
                             K[0:40, C_ID + r:C_ID + r + 1].to_broadcast([40, P]), negm[:],
                             start=True, stop=True)
                ins.then_inc(S["s_done"], 1)

            def values(h):
                w = wexp[:, h % 2]
                for d in range(2):
                    pe.wait_ge(S["p_done"], 2 * h + d + 1)
                    if h >= 1:
                        pe.wait_ge(S["num_free"], 2 * (h - 1) + d + 1)
                    for j in range(2):
                        blocks = [0, 1] + ([2] if j == 0 else [2, 3]) if d == 0 else \
                            [0, 1] + ([2, 3] if j == 0 else [3])
                        for i, b in enumerate(blocks):
                            ins = mm(ps[:, 6 + d, j * 256:j * 256 + DV + 1],
                                     w[:, d, b, j * P:(j + 1) * P], VX[:, b, h, :],
                                     start=i == 0, stop=i == len(blocks) - 1)
                        ins.then_inc(S["num_done"], 1)

            scores(0)
            for h in range(MH):
                if h + 1 < MH:
                    scores(h + 1)
                values(h)

            pe.wait_ge(S["y_ready"], 1)
            pe.wait_ge(S["num_free"], 2 * MH)
            for k in range(KB):
                if k >= 4:
                    pe.wait_ge(S["yT_ready"], k - 3)
                for b in range(TB):
                    ins = tr(ps[:, k % 4, b * P:(b + 1) * P], A[:, b, k * P:(k + 1) * P], ident)
                ins.then_inc(S["yT_psum"], 1)
            for i, r in enumerate((0, 32, 96, 64)):
                for n in range(4):
                    if i >= 1:
                        pe.wait_ge(S["bc_free"], 4 * (i - 1) + n + 1)
                    mm(ps[:, 4 + n, :], K[:, C_ID + r:C_ID + r + 1].to_broadcast([P, P]),
                       modrow[:, n * CH:(n + 1) * CH], start=True, stop=True
                       ).then_inc(S["bc_psum"], 1)

            pe.wait_ge(S["yT_ready"], KB)
            with pe.Fori(0, 2) as n2:
                for par in range(2):
                    for b in range(TB):
                        pe.wait_ge(S["out_free"], n2 * 4 + (2 * par + b + 1))
                    for kh in range(2):
                        pe.wait_ge(w_ld[kh], n2 * 32 + 16 * (16 + par + 1))
                        for b in range(TB):
                            for k in range(KH):
                                kk = kh * KH + k
                                ins = mm(ps[:, 2 * par + b, :], yT[:, kk, b * P:(b + 1) * P],
                                         W[kh][:, k, :], start=kk == 0, stop=kk == KB - 1)
                        ins.then_inc(S["w_free"], 1)

            pe.wait_ge(S["ld_keys"], 16)
            pe.wait_ge(S["out_free"], 4 + 8)
            pe.wait_ge(S["bc_free"], 12)
            pe.wait_ge(S["g2_ready"], 4)
            for i in range(2 * PH):
                tr(ps[:, i // 4, (i % 4) * P:(i % 4 + 1) * P], keys_raw[:, i, :], ident
                   ).then_inc(S["keys_psum"], 1)
            pe.wait_ge(S["h2_ready"], 2)
            for k in range(KB):
                if k >= 4:
                    pe.wait_ge(S["h2T_ready"], k - 3)
                for b in range(TB):
                    ins = tr(ps[:, 4 + k % 4, b * P:(b + 1) * P], A[:, b, k * P:(k + 1) * P], ident)
                ins.then_inc(S["h2T_psum"], 1)
            pe.wait_ge(S["h2T_ready"], KB)
            pe.wait_ge(S["keys_ready"], 4)

            for n in range(4):
                if n >= 2:
                    pe.wait_ge(S["q_free"], 4 * (n - 1))
                for kh in range(2):
                    pe.wait_ge(w_ld[kh], 16 * (20 + n + 1))
                    for j in range(4):
                        for k in range(KH):
                            kk = kh * KH + k
                            ins = mm(ps[:, 4 * (n % 2) + j, 0:T], W[kh][:, k, j * P:(j + 1) * P],
                                     h2T[:, kk, :], start=kk == 0, stop=kk == KB - 1)
                    ins.then_inc(S["w_free"], 1)
            pe.wait_ge(S["q_free"], KB)
            for b in range(TB):
                for i in range(2 * PH):
                    ins = mm(ps[:, 4 * b + i // 4, (i % 4) * P:(i % 4 + 1) * P],
                             qhT[:, i, b * P:(b + 1) * P], keysT[:, i, :], start=True, stop=True)
                    if i % 4 == 3:
                        ins.then_inc(S["score_psum"], 1)
            pe.wait_ge(S["score_ready"], 8)

            for b in range(TB):
                for n in range(4):
                    ins = mm(ps[:, 4 * b + n, :], zeros, K[:, 0:CH], start=True, stop=True)
                if b == 0:
                    ins.then_inc(S["pair_free"], 4)
                quads = PH * TOPK // 4
                with pe.Fori(b * quads, (b + 1) * quads) as q:
                    for s in range(4):
                        pe.wait_ge(S["diag_ready"], q * 4 + (s + 1))
                        pe.wait_ge(v_ld[s], q * 16 + 16)
                        for n in range(4):
                            ins = mm(ps[:, 4 * b + n, :], diag[:, s, :],
                                     ring[:, 4 + s, n * CH:(n + 1) * CH],
                                     start=False, stop=False, skip_group_check=True)
                        ins.then_inc(S["pair_free"], 1)

        @block.vector
        def _(dve):
            v = nc.vector
            link = chain(dve, "dve")
            v.memset(small[:, 0:1], 0.0).then_inc(S["moda_free"], 2)
            dve.wait_ge(S["vec_psum"], 1)
            v.tensor_copy(vec[:], ps[:, 7, 0:V_ALL]).then_inc(S["vec_ready"], 1)
            dve.wait_ge(S["std"], 1)
            v.reciprocal(st[:, 8:12], st[:, 4:8]).then_inc(S["rstd"], 1)
            dve.wait_ge(S["rstd"], 1)
            for i, tile in enumerate((B, A)):
                for b in range(TB):
                    v.tensor_scalar(tile[:, b, :], tile[:, b, :], st[:, 8 + 2 * i + b:9 + 2 * i + b],
                                    None, ALU.mult).then_inc(S["xn_ready"], 1)
            with dve.Fori(0, 4) as n2:
                for par in range(2):
                    dve.wait_ge(S["w_free"], n2 * 4 + (2 * par + 2))
                    v.tensor_copy(moda[:, bass.ds(n2 * (2 * CH) + par * CH, CH)], ps[0:2, par, :]
                                  ).then_inc(S["moda_free"], 1)
            dve.wait_ge(S["modcol_psum"], 1)
            dve.wait_ge(S["vec_ready"], 1)
            cols = ps[:, 7, 0:4 * KB].rearrange("p (a k c) -> p a c k", a=2, c=2)
            bias = vec[:, V_B:V_B + 32].rearrange("p (a k) -> p a k", a=2)
            for c_ in range(2):
                v.tensor_tensor(shT[:, c_, :], cols[:, 0, c_, :], bias[:, 0, :], ALU.add)
                link(v.tensor_tensor(gT[:, c_, :], cols[:, 1, c_, :], bias[:, 1, :], ALU.add))
                ins = v.scalar_tensor_tensor(out=gT[:, c_, :], in0=gT[:, c_, :], scalar=1.0,
                                             in1=vec[:, V_G:V_G + KB], op0=ALU.add, op1=ALU.mult)
                if c_ == 1:
                    ins.then_inc(S["mod_ready"], 1)
            dve.wait_ge(S["mod_ready"], 1)
            for k in range(1, KB, 2):
                dve.wait_ge(S["xT_psum"], k + 1)
                for side, c_ in ((0, 1), (1, 0)):
                    w = slice(side * T, (side + 1) * T)
                    ins = v.tensor_scalar(H[:, k, w], ps[:, k % 6, w], gT[:, c_, k:k + 1],
                                          shT[:, c_, k:k + 1], ALU.mult, ALU.add)
                ins.then_inc(S["ht_dve"], 1)

            def modb(m):
                for kh in range(2):
                    dve.wait_ge(m_ld[kh], 16 * (m + 1))
                    for k in range(KH):
                        kk = kh * KH + k
                        a = acc[:, m % 2, :]
                        s = vec[:, kk:kk + 1]
                        if kk == 0:
                            ins = v.tensor_scalar(a, W[2 + kh][:, k, :], s, None, ALU.mult)
                        else:
                            ins = v.scalar_tensor_tensor(out=a, in0=W[2 + kh][:, k, :], scalar=s,
                                                         in1=a, op0=ALU.mult, op1=ALU.add)
                        if k == KH - 1:
                            ins.then_inc(S["m_free"], 1)
                            dve.wait_ge(S["m_free"], 2 * m + kh + 1)
                        else:
                            link(ins)

            def modb_out(m):
                dve.wait_ge(S["modb_red"], m + 1)
                r = 32 * (m // 4)
                row = modrow[r:r + 1, (m % 4) * CH:(m % 4 + 1) * CH]
                v.tensor_tensor(row, ps[r:r + 1, 7, :], row, ALU.add).then_inc(S["modb_free"], 1)

            def conv_k(j):
                taps = vec[:, V_CONV + 9 * (4 + j):V_CONV + 9 * (5 + j)]
                link(v.tensor_scalar(KT[:, j, 0:T], kraw[:, j, 0:T], taps[:, 4:5], None, ALU.mult))
                link(v.scalar_tensor_tensor(out=KT[:, j, 1:T], in0=kraw[:, j, 0:T - 1],
                                            scalar=taps[:, 3:4], in1=KT[:, j, 1:T],
                                            op0=ALU.mult, op1=ALU.add))
                link(v.scalar_tensor_tensor(out=KT[:, j, 0:T - 1], in0=kraw[:, j, 1:T],
                                            scalar=taps[:, 5:6], in1=KT[:, j, 0:T - 1],
                                            op0=ALU.mult, op1=ALU.add))
                conv_grid(KT[:, j, T:2 * T], kraw[:, j, T:2 * T], taps, "kconv")

            def conv_grid(dst, src, taps, done):
                link(v.tensor_scalar(dst, src, taps[:, 4:5], None, ALU.mult))
                d = dst.rearrange("p (r w) -> p r w", r=ROWS)
                s = src.rearrange("p (r w) -> p r w", r=ROWS)
                around = [i for i in range(9) if i != 4]
                for i in around:
                    dr, dw = i // 3 - 1, i % 3 - 1
                    r0, r1 = max(0, -dr), ROWS - max(0, dr)
                    c0, c1 = max(0, -dw), GRID_W - max(0, dw)
                    o = d[:, r0:r1, c0:c1]
                    ins = v.scalar_tensor_tensor(out=o, in0=s[:, r0 + dr:r1 + dr, c0 + dw:c1 + dw],
                                                 scalar=taps[:, i:i + 1], in1=o,
                                                 op0=ALU.mult, op1=ALU.add)
                    if i == around[-1]:
                        ins.then_inc(S[done], 1)
                    else:
                        link(ins)

            def gates():
                fg = t1
                dve.wait_ge(S["proj_free"], 1)
                link(v.tensor_copy(fg[:], gsb[64:104, :]))
                link(v.scalar_tensor_tensor(out=t2[:], in0=fg[:], scalar=-1.0, in1=fg[:],
                                            op0=ALU.mult, op1=ALU.max))
                v.tensor_scalar(t1[:], fg[:], 0.0, None, ALU.min).then_inc(S["abs_ready"], 1)

            def scans():
                dve.wait_ge(S["ln_ready"], 1)
                link(v.tensor_tensor(t1[:], t1[:], t2[:], ALU.subtract))
                link(v.memset(t2[:], 0.0))
                one = lambda r, n: K[r:r + MH, C_ONE:C_ONE + 1].to_broadcast([MH, n])
                c_rev = slice(T - 1, None, -1)
                l_rev = slice(2 * T - 1, T - 1, -1)
                link(v.tensor_tensor_scan(t2[0:8, :], one(0, 2 * T), t1[0:8, :], 0.0,
                                          ALU.mult, ALU.add))
                link(v.tensor_tensor_scan(t2[32:40, c_rev], one(32, T), t1[32:40, c_rev], 0.0,
                                          ALU.mult, ALU.add))
                link(v.tensor_tensor_scan(t2[32:40, l_rev], one(32, T), t1[32:40, l_rev],
                                          t2[32:40, 0:1], ALU.mult, ALU.add))
                u = gsb[0:40, :]
                v.tensor_tensor(u, u, t2[:], ALU.subtract).then_inc(S["u_ready"], 1)
                dve.wait_ge(S["u_ready"], 1)
                link(v.memset(t1[:], 0.0))
                link(v.tensor_tensor_scan(t1[0:8, :], u[0:8, :], u[0:8, :], 0.0, ALU.max, ALU.max))
                link(v.tensor_tensor_scan(t1[32:40, c_rev], u[32:40, c_rev], u[32:40, c_rev], 0.0,
                                          ALU.max, ALU.max))
                link(v.tensor_tensor_scan(t1[32:40, l_rev], u[32:40, l_rev], u[32:40, l_rev],
                                          t1[32:40, 0:1], ALU.max, ALU.max))
                v.tensor_scalar(negm[:], t1[:, T:2 * T], -1.0, None, ALU.mult)
                v.tensor_tensor(t2[:, T:2 * T], t2[:, T:2 * T], t1[:, T:2 * T], ALU.add
                                ).then_inc(S["thr_in"], 1)

            dve.wait_ge(S["ld_bm"], 64)
            jobs = {3: lambda: (dve.wait_ge(S["proj_free"], 5), gates(), conv_k(0)),
                    4: lambda: conv_k(1), 5: lambda: conv_k(2), 6: lambda: conv_k(3)}
            for j in range(4):
                jobs[7 + j] = lambda j=j: (dve.wait_ge(S["proj_free"], 9), conv_grid(
                    QT[:, j, :], qraw[:, j, :], vec[:, V_CONV + 9 * j:V_CONV + 9 * (j + 1)], "qconv"))
            for m in range(MODB):
                modb(m)
                if m >= 1:
                    modb_out(m - 1)
                if m in jobs:
                    jobs[m]()
            modb_out(MODB - 1)
            scans()
            dve.wait_ge(S["uT_psum"], 1)
            v.tensor_copy(uT[:], ps[:, 6, 0:240].rearrange("p (b r) -> p b r", b=6)
                          ).then_inc(S["uT_ready"], 1)
            dve.wait_ge(S["uT_ready"], 1)

            def diagonals(h):
                dve.wait_ge(S["s_done"], h + 1)
                if h >= 2:
                    dve.wait_ge(S["num_done"], 4 * (h - 1))
                for d in range(2):
                    for b in range(2):
                        w = wexp[:, h % 2, d, 2 + b, b * P:(b + 1) * P]
                        ins = v.scalar_tensor_tensor(
                            out=w, in0=ps[:, 4 + h % 2, d * T + b * P:d * T + (b + 1) * P],
                            scalar=uT[:, 2 + b, 32 * d + h:32 * d + h + 1],
                            in1=K[:, C_MASK + d * P:C_MASK + (d + 1) * P], op0=ALU.add, op1=ALU.add)
                    ins.then_inc(S["diag_in"], 1)

            def weigh(h):
                for d in range(2):
                    dve.wait_ge(S["exp_done"], 2 * h + d + 1)
                    w = flat2(wexp[:, h % 2, d])
                    runs = [(0, 768), (896, 1024)] if d == 0 else [(0, 640), (768, 1024)]
                    parts = []
                    for a, z in runs:
                        parts += [(a, min(z, 512)), (512, z)] if a < 512 < z else [(a, z)]
                    for a, z in parts:
                        bank = 2 * (h % 2) + a // 512
                        ins = v.scalar_tensor_tensor(
                            out=w[:, a:z], in0=ps[:, bank, a % 512:(z - 1) % 512 + 1],
                            scalar=DK ** -0.5, in1=w[:, a:z], op0=ALU.mult, op1=ALU.mult)
                    ins.then_inc(S["p_done"], 1)

            def flat2(ap):
                return ap.rearrange("p s j -> p (s j)")

            def divide(h):
                for d in range(2):
                    dve.wait_ge(S["num_done"], 4 * h + 2 * d + 2)
                    num = ps[:, 6 + d, :].rearrange("p (j n) -> p j n", j=2)
                    den = num[:, :, DV:DV + 1]
                    r = 32 * d + h
                    q = small[:, 4 + 2 * d:6 + 2 * d].unsqueeze(2)
                    link(v.tensor_copy(q, den))
                    link(v.scalar_tensor_tensor(out=q, in0=q, scalar=-1.0, in1=q,
                                                op0=ALU.mult, op1=ALU.max))
                    link(v.tensor_tensor(q, q, uT[:, 4:6, r:r + 1], ALU.max))
                    link(v.reciprocal(q, q))
                    for j in range(2):
                        o = hm[:, j, h * DV:(h + 1) * DV]
                        s = small[:, 4 + 2 * d + j:5 + 2 * d + j]
                        if d == 0:
                            ins = v.tensor_scalar(o, num[:, j, 0:DV], s, None, ALU.mult)
                        else:
                            ins = v.scalar_tensor_tensor(out=o, in0=num[:, j, 0:DV], scalar=s, in1=o,
                                                         op0=ALU.mult, op1=ALU.add)
                    ins.then_inc(S["num_free"], 1)
                    dve.wait_ge(S["num_free"], 2 * h + d + 1)

            diagonals(0)
            for h in range(MH):
                if h + 1 < MH:
                    diagonals(h + 1)
                weigh(h)
                divide(h)

            dve.wait_ge(S["fn2_free"], 2 * FG)
            for b in range(TB):
                sq = tmp[:, 4096 + b * FW:4096 + (b + 1) * FW]
                link(v.tensor_tensor(sq, hm[:, b, :], hm[:, b, :], ALU.mult))
                ins = v.reduce_sum(st[:, 16 + b * MH:16 + (b + 1) * MH],
                                   sq.rearrange("p (h d) -> p h d", h=MH), AX_X)
            ins.then_inc(S["hsq"], 1)
            dve.wait_ge(S["std"], 2)
            link(v.reciprocal(st[:, 32:56], st[:, 32:56]))
            dve.wait_ge(S["o_sig"], 1)
            dve.wait_ge(S["ld_gy"], 32)
            for b in range(TB):
                for g in range(FG):
                    a = A[:, b, g * GW:(g + 1) * GW]
                    v.scalar_tensor_tensor(out=a, in0=a, scalar=st[:, 32 + b * FG + g:33 + b * FG + g],
                                           in1=gy[:, g * GW:(g + 1) * GW], op0=ALU.mult, op1=ALU.mult)
                link(v.tensor_tensor(A[:, b, FW:D], A[:, b, FW:D], gy[:, FW:D], ALU.mult))
                for h in range(MH):
                    a = A[:, b, FW + h * DV:FW + (h + 1) * DV]
                    ins = v.scalar_tensor_tensor(out=a, in0=hm[:, b, h * DV:(h + 1) * DV],
                                                 scalar=st[:, 40 + b * MH + h:41 + b * MH + h], in1=a,
                                                 op0=ALU.mult, op1=ALU.mult)
            ins.then_inc(S["y_ready"], 1)
            v.memset(small[:, 1:2], 0.0).then_inc(S["out_free"], 4)

            dve.wait_ge(S["ld_gffn"], 16)
            for n in range(4):
                dve.wait_ge(S["bc_psum"], 12 + n + 1)
                o = g2[:, n * CH:(n + 1) * CH]
                v.scalar_tensor_tensor(out=o, in0=ps[:, 4 + n, :], scalar=1.0, in1=o, op0=ALU.add,
                                       op1=ALU.mult).then_inc(S["g2_ready"], 1)

            dve.wait_ge(S["ld_x2"], 16)
            dve.wait_ge(S["bc_free"], 12)
            dve.wait_ge(S["g2_ready"], 4)
            for n in range(4):
                dve.wait_ge(S["w_free"], 32 + 2 * n + 2)
                for b in range(TB):
                    o = B[:, b, n * CH:(n + 1) * CH]
                    t = cand[:, b * CH:(b + 1) * CH]
                    v.tensor_tensor(t, ps[:, 2 * (n % 2) + b, :], ga1[:, n * CH:(n + 1) * CH],
                                    ALU.mult).then_inc(S["out_free"], 1)
                    dve.wait_ge(S["out_free"], 4 + 2 * n + b + 1)
                    v.tensor_tensor(o, o, t, ALU.add).then_inc(S["x1_ready"], 1)

            dve.wait_ge(S["std2"], 1)
            link(v.reciprocal(st[:, 4:6], st[:, 2:4]))
            for b in range(TB):
                link(v.scalar_tensor_tensor(out=A[:, b, :], in0=B[:, b, :], scalar=st[:, 4 + b:5 + b],
                                            in1=g2, op0=ALU.mult, op1=ALU.mult))
                v.tensor_tensor(A[:, b, :], A[:, b, :], sh2, ALU.add).then_inc(S["h2_ready"], 1)

            iota = K[:, C_IOTA:C_IOTA + TOPK]

            def top16(values, indices, src, scratch):
                link(v.max(values[:, 0:8], src))
                v.max_index(indices[:, 0:8], values[:, 0:8], src)
                link(v.match_replace(scratch, values[:, 0:8], src, LOWEST))
                link(v.max(values[:, 8:16], scratch))
                v.max_index(indices[:, 8:16], values[:, 8:16], scratch)

            for b in range(TB):
                for i in range(2 * PH):
                    dve.wait_ge(S["score_ready"], 4 * b + i // 4 + 1)
                    top16(sv[:, 16 * i:16 * i + 16], siu[:, 16 * i:16 * i + 16], sc[:, b, i, :],
                          work[:, i * NK:(i + 1) * NK])
                link(v.memset(small[:, 2:3], 0.0))
                link(v.tensor_copy(si, siu))
                halves = lambda t: t.rearrange("p (h two k) -> p h two k", two=2, k=TOPK)
                svh, sih = halves(sv), halves(si)
                sq = lambda t: t.rearrange("p (h a c) -> p h a c", h=PH, a=TOPK)
                full = [P, PH, TOPK, TOPK]
                link(v.tensor_tensor(sq(cand), svh[:, :, 0, :].unsqueeze(3).to_broadcast(full),
                                     svh[:, :, 1, :].unsqueeze(2).to_broadcast(full), ALU.add))
                for h in range(PH):
                    top16(top[:, 16 * h:16 * h + 16], pos[:, 16 * h:16 * h + 16],
                          cand[:, h * 256:(h + 1) * 256], work[:, h * 256:(h + 1) * 256])
                link(v.memset(small[:, 2:3], 0.0))
                for p_ in range(2):
                    op, k = (ALU.logical_shift_right, 4) if p_ == 0 else (ALU.bitwise_and, 15)
                    link(v.tensor_scalar(half, pos, k, None, op))
                    link(v.tensor_copy(halff, half))
                    link(v.tensor_tensor(sq(work), sq3(halff).unsqueeze(3).to_broadcast(full),
                                         iota.unsqueeze(1).unsqueeze(1).to_broadcast(full),
                                         ALU.is_equal))
                    link(v.tensor_tensor(sq(work), sq(work),
                                         sih[:, :, p_, :].unsqueeze(2).to_broadcast(full), ALU.mult))
                    link(v.reduce_sum(sel[:, p_ * P:(p_ + 1) * P],
                                      work.rearrange("p (k a) -> p k a", a=TOPK), AX_X))
                link(v.scalar_tensor_tensor(out=eflt, in0=sel[:, 0:P], scalar=float(NK),
                                            in1=sel[:, P:2 * P], op0=ALU.mult, op1=ALU.add))
                link(v.tensor_copy(eidx[:, b * P:(b + 1) * P], eflt))
                gb = gate[:, b * P:(b + 1) * P]
                v.tensor_tensor(sq3(gb), sq3(top), sq3(top)[:, :, 0:1].to_broadcast([P, PH, TOPK]),
                                ALU.subtract).then_inc(S["top_in"], 1)
                dve.wait_ge(S["gate_e"], b + 1)
                link(v.reduce_sum(sums[:, 0:PH], sq3(gb), AX_X))
                link(v.reciprocal(sums[:, 8:8 + PH], sums[:, 0:PH]))
                link(v.tensor_tensor(sq3(gb), sq3(gb), sums[:, 8:8 + PH].unsqueeze(2).to_broadcast(
                    [P, PH, TOPK]), ALU.mult))
            v.memset(small[:, 2:3], 0.0).then_inc(S["peer_in"], 1)
            v.memset(small[:, 3:4], 0.0).then_inc(S["u_free"], 4)

            for b in range(TB):
                with dve.Fori(b * PH, (b + 1) * PH) as g:
                    for r in range(TOPK):
                        s = r % 4
                        dve.wait_ge(u_ld[s], g * 64 + 16 * (r // 4 + 1))
                        v.scalar_tensor_tensor(
                            out=ring[:, s, :], in0=ring[:, s, :], scalar=1.0, in1=A[:, b, :],
                            op0=ALU.mult, op1=ALU.mult,
                            accum_out=dots[:, bass.ds(g * TOPK + r, 1)]).then_inc(S["u_free"], 1)
                    dve.wait_ge(S["u_free"], g * TOPK + (TOPK + 4))
                    v.memset(small[:, 2:3], 0.0).then_inc(S["dots_ready"], 1)
                    dve.wait_ge(S["gelu_done"], g + 1)
                    v.tensor_tensor(wgt[:, bass.ds(g * TOPK, TOPK)], act_t[:, bass.ds(g * TOPK, TOPK)],
                                    gate[:, bass.ds(g * TOPK, TOPK)], ALU.mult
                                    ).then_inc(S["wgt_ready"], 1)

            for b in range(TB):
                dve.wait_ge(S["pair_free"], 4 + P * (b + 1))
                for n in range(4):
                    t = ring[:, b, n * CH:(n + 1) * CH]
                    ins = v.tensor_tensor(t, ps[:, 4 * b + n, :], ga2[:, n * CH:(n + 1) * CH], ALU.mult)
                link(ins)
                v.tensor_tensor(B[:, b, :], B[:, b, :], ring[:, b, :], ALU.add).then_inc(S["ssq3"], 1)
            dve.wait_ge(S["std3"], 1)
            dve.wait_ge(S["ld_gfin"], 16)
            link(v.reciprocal(st[:, 4:6], st[:, 2:4]))
            for b in range(TB):
                ins = v.scalar_tensor_tensor(out=B[:, b, :], in0=B[:, b, :], scalar=st[:, 4 + b:5 + b],
                                             in1=gy[:], op0=ALU.mult, op1=ALU.mult)
            ins.then_inc(S["final_ready"], 1)


def sq3(t):
    return t.rearrange("p (h k) -> p h k", k=TOPK)


INPUTS = ["x", "c", "ctx", "c_ctx", "w_mod", "b_mod", "g_norm_mix", "g_norm_ffn", "w_in", "b_gate",
          "conv_qk", "g_fourier", "g_mlstm", "w_out", "w_query", "sub_keys", "expert_u", "expert_v",
          "g_final"]


def kernel(**inputs):
    from concourse import bacc
    from concourse.bass_utils import run_bass_kernel_spmd

    nc = bacc.Bacc("TRN2", target_bir_lowering=False, num_devices=1)
    arrays = {f"in_{n}": np.ascontiguousarray(inputs[n]) for n in INPUTS}
    arrays["in_consts"] = constants()
    args = [nc.dram_tensor(n, a.shape, mybir.dt.from_np(a.dtype), kind="ExternalInput").ap()
            for n, a in arrays.items()]
    out = nc.dram_tensor("out_x", (1, T, D), F32, kind="ExternalOutput").ap()
    build(nc, *args, out)
    result = run_bass_kernel_spmd(nc, [arrays], core_ids=[0])
    return result.results[0]["out_x"]
```

```python
from contextlib import ExitStack

import numpy as np

import concourse.bass as bass
from concourse import mybir
from concourse.alu_op_type import AluOpType as ALU

F32 = mybir.dt.float32
U32 = mybir.dt.uint32
ACT = mybir.ActivationFunctionType
AX_X = mybir.AxisListType.X

P = 128
D = 2048
KB = D // P
T = 256
TB = T // P
GRID_W = 64
ROWS = T // GRID_W
CH = 512
KH = KB // 2
FW = D // 2
FG = 4
GW = FW // FG
MH = 8
DV = 128
DK = 64
EPS = 1e-6
PH = 8
NK = 128
TOPK = 16
FAR = -1e30
LOWEST = -3e38
FN_BANKS = ((0, 1), (5, 6))
REDUCE_BEHIND = [3, 5, 7, 11, 15, 17, 19, 21, 24, 26]
J0 = 4
PICK_STEPS = 24

C_ID = 0
C_DFT = C_ID + P
C_MASK = C_DFT + 2 * CH
C_IOTA = C_MASK + 2 * P
C_ONE = C_IOTA + 16
C_EPS = C_ONE + 32
C_ZERO = C_EPS + 1
C_ALL = C_ZERO + P + 15

V_C = 0
V_B = 32
V_G = 64
V_CONV = 80
V_ALL = V_CONV + 72

W_IN_CHUNKS = [3, 2, 4, 5, 0, 1, 6, 7]
GATE_ROWS = [0, 64, 32, 96]
NG = 104
MODB = 16
MODB_EARLY, MODB_LATE = 2, 12


def constants():
    c = np.zeros((P, C_ALL), np.float32)
    c[:, C_ID:C_ID + P] = np.eye(P)
    for b in range(2):
        a = 2 * np.pi * ((np.outer(b * P + np.arange(P), np.arange(T))) % T) / T
        c[:, C_DFT + b * CH:C_DFT + b * CH + T] = np.cos(a)
        c[:, C_DFT + b * CH + T:C_DFT + (b + 1) * CH] = np.sin(a)
    s, j = np.meshgrid(np.arange(P), np.arange(P), indexing="ij")
    c[:, C_MASK:C_MASK + P] = np.where(s <= j, 0.0, FAR)
    c[:, C_MASK + P:C_MASK + 2 * P] = np.where(s >= j, 0.0, FAR)
    c[:, C_IOTA:C_IOTA + 16] = np.arange(16)
    c[:, C_ONE:C_ONE + 32] = 1.0
    c[:, C_EPS] = EPS
    return c


def build(nc, x, c, ctx, c_ctx, w_mod, b_mod, g_norm_mix, g_norm_ffn, w_in, b_gate, conv_qk,
          g_fourier, g_mlstm, w_out, w_query, sub_keys, expert_u, expert_v, g_final, consts, out):
    with ExitStack() as stack:
        def sb(name, shape, dt=F32):
            return stack.enter_context(nc.sbuf_tensor(name, shape, dt))

        def sem(name):
            return stack.enter_context(nc.semaphore(name))

        ps = stack.enter_context(nc.psum_tensor("ps", [P, 8, CH], F32))
        ring = sb("ring", [P, 8, D])
        A = sb("A", [P, TB, D])
        B = sb("B", [P, TB, D])
        H = sb("H", [P, KB, CH])
        KT = sb("KT", [P, 4, 2 * T])
        QT = sb("QT", [P, 4, T])
        VX = sb("VX", [P, 4, MH, DV + 1])
        modrow = sb("modrow", [P, D])
        gy = sb("gy", [P, D])
        K = sb("K", [P, C_ALL])
        wg = sb("wg", [P, KB, NG])
        acc = sb("acc", [P, 2, CH])
        qh = sb("qh", [P, 2, 4, T])
        vec = sb("vec", [P, V_ALL])
        shT = sb("shT", [P, 2, KB])
        gT = sb("gT", [P, 2, KB])
        gsb = sb("gsb", [NG, 2 * T])
        t1 = sb("t1", [40, 2 * T])
        t2 = sb("t2", [40, 2 * T])
        negm = sb("negm", [40, T])
        bg = sb("bg", [NG, 1])
        uT = sb("uT", [P, 6, 40])
        st = sb("st", [P, 64])
        small = sb("small", [P, 16])

        ident = K[:, C_ID:C_ID + P]
        ones32 = K[:, C_ONE:C_ONE + 32]
        eps = K[:, C_EPS:C_EPS + 1]
        zeros = K[:, C_ZERO:C_ZERO + P]
        dft = K[:, C_DFT:C_DFT + 2 * CH].rearrange("p (b n) -> p b n", b=2)
        flat = lambda t: t[:].rearrange("p a b -> p (a b)")
        ringf, Hf, KTf, QTf = flat(ring), flat(H), flat(KT), flat(QT)
        VXf = VX[:].rearrange("p a b c -> p (a b c)")
        W = [ringf[:, i * KH * CH:(i + 1) * KH * CH].rearrange("p (k n) -> p k n", k=KH)
             for i in range(4)]
        rows = flat(acc)[0:32, 0:3 * P]
        moda = VXf[0:2, 0:2 * D]
        conv_rows = QTf[0:9, 0:2 * CH]
        kraw = B[:, 0, :].rearrange("p (j t) -> p j t", j=4)
        qraw = B[:, 1, 0:4 * T].rearrange("p (j t) -> p j t", j=4)
        wexp = B[:, 0, :].rearrange("p (d s j) -> p d s j", d=2, s=4)
        hm = B[:, 1, :].rearrange("p (b n) -> p b n", b=2)
        pts = Hf[:, 6144:8192].rearrange("p (r b n) -> p r b n", r=2, b=2)
        tmp = ringf[:, 0:4 * D]
        yT = Hf[:, 0:4096].rearrange("p (k t) -> p k t", k=KB)
        ga1, sh2 = Hf[:, 4096:6144], Hf[:, 6144:8192]
        ga2 = KTf[:, 0:D]
        g2 = VXf[:, 0:D]
        h2T = yT
        keys_raw = gy[:].rearrange("p (h n) -> p h n", h=2 * PH)
        keysT = modrow[:].rearrange("p (h n) -> p h n", h=2 * PH)
        sc = Hf[:, 4096:8192]
        xtmp = QTf[:, 0:2 * CH]
        stage = QTf[:, 0:2 * NK]
        cand, work = QTf[:, 256:512], QTf[:, 512:768]
        siu, pos, half = (QTf[:, a:z].bitcast(U32) for a, z in ((768, 800), (800, 816), (816, 832)))
        halff, sv, si = QTf[:, 832:848], QTf[:, 848:880], QTf[:, 880:912]
        top, sel, eflt = QTf[:, 912:928], QTf[:, 928:960], QTf[:, 960:976]
        topd, dots, wgt, act_t, soft = (VXf[:, D + 256 * i:D + 256 * (i + 1)] for i in range(5))
        sums = VXf[:, D + 1280:D + 1296]
        eidx = flat(acc)[:, 0:256].bitcast(U32)
        wgf = flat(wg)
        diag = wgf[:, 0:4 * P].rearrange("p (s n) -> p s n", s=4)
        slot_idx = wgf[:, 4 * P:4 * P + 8].bitcast(U32)

        names = """picked pick_step sums_inv ld_const ld_c ld_rows ld_x ld_ctx ld_wg ld_bg ld_gy ld_bm
        ld_x2 ld_gffn ld_keys ld_gfin wg_zero modrow_zero silu_c vec_psum vec_ready moda_free
        modcol_psum mod_ready ssq std rstd xn_ready xT_psum ht_act ht_dve w_free m_free modb_red
        modb_free proj_free gates_psum abs_ready ln_ready thr_in thr_ready u_ready uT_psum
        uT_ready kconv qconv k_ready q_ready ones_v fn1_done fn1_free fn2_done fn2_free s_done
        diag_in exp_done p_done num_done num_free y_ready yT_psum yT_ready bc_psum bc_free
        g2_ready o_sig hsq out_free x1_ready ssq2 std2 h2_ready h2T_psum h2T_ready keys_psum
        keys_ready q_free score_psum score_ready u_free pair_free dots_ready gelu_done wgt_ready
        diag_ready copied ssq3 std3 final_ready stored dve act""".split()
        S = {n: sem(n) for n in names}
        w_ld = [sem(f"w_ld{i}") for i in range(2)]
        m_ld = [sem(f"m_ld{i}") for i in range(2)]
        u_ld = [sem(f"u_ld{i}") for i in range(4)]
        v_ld = [sem(f"v_ld{i}") for i in range(4)]

        def chain(engine, name):
            count = [0]

            def link(ins):
                count[0] += 1
                ins.then_inc(S[name], 1)
                engine.wait_ge(S[name], count[0])
            return link

        def dve_chain(engine):
            def steps(n):
                count = [0]

                def step(ins):
                    count[0] += 1
                    assert count[0] <= PICK_STEPS
                    ins.then_inc(S["pick_step"], 1)
                    engine.wait_ge(S["pick_step"], n * PICK_STEPS + count[0])
                return step
            return steps

        block = stack.enter_context(nc.Block())

        @block.sync
        def _(sp):
            sp.dma_start(K[:], consts).then_inc(S["ld_const"], 16)

            def load(piece, src, kh, n0):
                sp.dma_start(W[piece % 2], src[kh * KH * P:(kh + 1) * KH * P, n0].rearrange(
                    "(k p) n -> p k n", p=P)).then_inc(w_ld[piece % 2], 16)

            wm, wi = w_mod[0], w_in[0]
            for kh in range(2):
                load(kh, wm, kh, bass.ds(0, CH))
            sp.dma_start(A[:], x[0].rearrange("(b p) d -> p b d", p=P)).then_inc(S["ld_x"], 16)
            sp.dma_start(B[:], ctx[0].rearrange("(b p) d -> p b d", p=P)).then_inc(S["ld_ctx"], 16)
            with sp.Fori(1, 8) as n:
                for kh in range(2):
                    sp.wait_ge(S["w_free"], n * 2 + (kh - 1))
                    load(kh, wm, kh, bass.ds(n * CH, CH))
            for i, n in enumerate(W_IN_CHUNKS):
                for kh in range(2):
                    sp.wait_ge(S["w_free"], 16 + 2 * i + kh - 1)
                    load(kh, wi, kh, bass.ds(n * CH, CH))
            sp.wait_ge(S["y_ready"], 1)
            for base, src in ((32, w_out[0]), (40, w_query[0])):
                with sp.Fori(0, 4) as n:
                    for kh in range(2):
                        sp.wait_ge(S["w_free"], n * 2 + (base + kh - 1))
                        load(kh, src, kh, bass.ds(n * CH, CH))
            for b in range(TB):
                sp.wait_ge(S["final_ready"], b + 1)
                sp.dma_start(out[0, b * P:(b + 1) * P, :], B[:, b, :]).then_inc(S["stored"], 16)
            sp.wait_ge(S["stored"], 16 * TB)

        @block.gpsimd
        def _(pool):
            nc.gpsimd.memset(wg[:], 0.0).then_inc(S["wg_zero"], 1)
            nc.gpsimd.memset(bg[:], 0.0).then_inc(S["wg_zero"], 1)
            nc.gpsimd.memset(modrow[:], 0.0).then_inc(S["modrow_zero"], 1)
            pool.wait_ge(S["wg_zero"], 2)
            gates0 = 8 * CH
            for g, r in enumerate(GATE_ROWS):
                pool.dma_start(wg[:, :, r:r + MH],
                               w_in[0][:, gates0 + g * MH:gates0 + (g + 1) * MH].rearrange(
                                   "(k p) n -> p k n", p=P)).then_inc(S["ld_wg"], 16)
                pool.dma_start(bg[r:r + MH, :], b_gate[0:1, g * MH:(g + 1) * MH].rearrange(
                    "a n -> n a")).then_inc(S["ld_bg"], 16)
            pool.wait_ge(S["modrow_zero"], 1)
            for r in range(4):
                pool.dma_start(modrow[32 * r:32 * r + 1, :], b_mod[0:1, (2 + r) * D:(3 + r) * D]
                               ).then_inc(S["ld_bm"], 16)
            pool.dma_start(gy[:, 0:FW], g_fourier.to_broadcast([P, FW])).then_inc(S["ld_gy"], 16)
            pool.dma_start(gy[:, FW:D], g_mlstm.to_broadcast([P, FW])).then_inc(S["ld_gy"], 16)

            pool.wait_ge(S["w_free"], 11)
            wm = w_mod[0]

            def load(m, kh):
                pool.dma_start(W[2 + kh], wm[kh * KH * P:(kh + 1) * KH * P,
                                             bass.ds(m * CH + 2 * D, CH)].rearrange(
                    "(k p) n -> p k n", p=P)).then_inc(m_ld[kh], 16)
            for kh in range(2):
                load(0, kh)

            def load_from(m0, m1):
                with pool.Fori(m0, m1) as m:
                    for kh in range(2):
                        pool.wait_ge(S["m_free"], m * 2 + (kh - 1))
                        load(m, kh)
            load_from(1, MODB_LATE + 1)
            pool.wait_ge(S["num_done"], 4 * MH)
            pool.dma_start(g2, g_norm_ffn.to_broadcast([P, D])).then_inc(S["ld_gffn"], 16)
            pool.wait_ge(S["y_ready"], 1)
            pool.dma_start(B[:], x[0].rearrange("(b p) d -> p b d", p=P)).then_inc(S["ld_x2"], 16)
            pool.dma_start(keys_raw, sub_keys[0].rearrange("h p n d -> n (h p) d")
                           ).then_inc(S["ld_keys"], 16)
            load_from(MODB_LATE + 1, MODB)
            pool.wait_ge(S["keys_psum"], 16)
            pool.dma_start(gy[:], g_final.rearrange("(a d) -> a d", a=1).to_broadcast([P, D])
                           ).then_inc(S["ld_gfin"], 16)

            def gather(table, slot, rank, index, count, loaded):
                nc.gpsimd.tensor_copy(index, eidx[:, bass.ds(rank, 1)]).then_inc(S["copied"], 1)
                pool.wait_ge(S["copied"], count)
                pool.nop(nofuse=True)
                nc.gpsimd.indirect_dma_start(
                    ring[:, slot, :], None, table, bass.IndirectOffsetOnAxis(ap=index, axis=0)
                ).then_inc(loaded, 16)

            def gather_u(rank, s, count):
                pool.wait_ge(S["u_free"], rank + 1)
                gather(expert_u[0], 4 + s, rank, slot_idx[:, s:s + 1], count, u_ld[s])

            def gather_v(rank, s, count):
                pool.wait_ge(S["pair_free"], rank + 1)
                gather(expert_v[0], s, rank, slot_idx[:, 4 + s:5 + s], count, v_ld[s])

            quads = TOPK // 4
            pool.wait_ge(S["picked"], 1)
            with pool.Fori(0, quads) as q:
                for s in range(4):
                    gather_u(q * 4 + s, s, q * 4 + (s + 1))
            pool.wait_ge(S["w_free"], 48)
            with pool.Fori(1, TB * PH) as g:
                pool.wait_ge(S["picked"], g + 1)
                pool.nop(nofuse=True)
                with pool.Fori(0, quads) as q:
                    for s in range(4):
                        done = g * 32 + q * 8 + (2 * s - 16)
                        gather_u(g * TOPK + q * 4 + s, s, done + 1)
                        gather_v(g * TOPK + q * 4 + (s - TOPK), s, done + 2)
            with pool.Fori(0, quads) as q:
                for s in range(4):
                    last = (TB * PH - 1) * TOPK
                    gather_v(q * 4 + (last + s), s, q * 4 + (2 * last + TOPK + s + 1))

        @block.scalar
        def _(act):
            link = chain(act, "act")
            nc_a = nc.scalar

            def fnet_out(g):
                act.wait_ge(S["fn2_done"], g + 1)
                for b in range(TB):
                    src = ps[:, (2, 7)[g % 2], b * T:(b + 1) * T]
                    nc_a.copy(A[:, b, g * GW:(g + 1) * GW], src)
                    nc_a.activation(tmp[:, (g * 2 + b) * GW:(g * 2 + b + 1) * GW], src, ACT.Square,
                                    accum_out=st[:, 8 + b * FG + g:9 + b * FG + g]
                                    ).then_inc(S["fn2_free"], 1)

            act.dma_start(rows[0:KB, 0:P], c[0].rearrange("(k p) -> k p", p=P)).then_inc(S["ld_c"], 16)
            act.dma_start(rows[KB:2 * KB, 0:P], c_ctx.rearrange("(k p) -> k p", p=P)
                          ).then_inc(S["ld_c"], 16)
            act.dma_start(rows[0:32, P:2 * P], b_mod[0, 0:2 * D].rearrange("(k p) -> k p", p=P)
                          ).then_inc(S["ld_rows"], 16)
            act.dma_start(rows[0:KB, 2 * P:3 * P], g_norm_mix[0].rearrange("(k p) -> k p", p=P)
                          ).then_inc(S["ld_rows"], 16)
            act.dma_start(conv_rows, conv_qk[0].rearrange("a b n -> (a b) n")
                          ).then_inc(S["ld_rows"], 16)
            act.wait_ge(S["ld_c"], 32)
            nc_a.activation(rows[:, 0:P], rows[:, 0:P], ACT.Silu).then_inc(S["silu_c"], 1)

            act.wait_ge(S["ld_const"], 16)
            for i, (tile, loaded) in enumerate(((B, "ld_ctx"), (A, "ld_x"))):
                act.wait_ge(S[loaded], 16)
                for b in range(TB):
                    o = (2 * i + b) * D
                    nc_a.activation(Hf[:, o:o + D], tile[:, b, :], ACT.Square,
                                    accum_out=st[:, 2 * i + b:2 * i + b + 1]).then_inc(S["ssq"], 1)
            act.wait_ge(S["ssq"], 4)
            nc_a.activation(st[:, 4:8], st[:, 0:4], ACT.Sqrt, bias=eps, scale=1.0 / D
                            ).then_inc(S["std"], 1)

            act.wait_ge(S["mod_ready"], 1)
            for k in range(0, KB, 2):
                act.wait_ge(S["xT_psum"], k + 1)
                for side, c_ in ((0, 1), (1, 0)):
                    cols = slice(side * T, (side + 1) * T)
                    ins = nc_a.activation(H[:, k, cols], ps[:, k % 6, cols], ACT.Identity,
                                          bias=shT[:, c_, k:k + 1], scale=gT[:, c_, k:k + 1])
                ins.then_inc(S["ht_act"], 1)

            act.wait_ge(S["ld_bg"], 64)
            act.wait_ge(S["gates_psum"], 1)
            nc_a.activation(gsb[:], ps[0:NG, 0, :], ACT.Identity, bias=bg[:]
                            ).then_inc(S["proj_free"], 1)
            group = 1
            for i, n in enumerate(W_IN_CHUNKS[:4]):
                act.wait_ge(S["w_free"], 16 + 2 * (i + 1))
                for j in range(4):
                    bank = ps[:, group % 7, :]
                    if n == 3:
                        dst, src = kraw[:, j, :], bank
                    elif n == 2:
                        dst, src = qraw[:, j, :], bank[:, 0:T]
                    else:
                        h0 = (n - 4) * 4
                        dst = VX[:, j, h0:h0 + 4, 0:DV]
                        src = bank.rearrange("p (h d) -> p h d", h=4)
                    nc_a.copy(dst, src).then_inc(S["proj_free"], 1)
                    group += 1
                if n == 2:
                    act.wait_ge(S["abs_ready"], 1)
                    link(nc_a.activation(t2[:], t2[:], ACT.Exp, scale=-1.0))
                    nc_a.activation(t2[:], t2[:], ACT.Ln, bias=K[0:40, C_ONE:C_ONE + 1]
                                    ).then_inc(S["ln_ready"], 1)
            for b in range(4):
                ins = nc_a.activation(VX[:, b, :, DV:DV + 1], K[:, C_ONE:C_ONE + MH].unsqueeze(2),
                                      ACT.Copy)
            ins.then_inc(S["ones_v"], 1)

            for j in range(4):
                act.wait_ge(S["kconv"], j + 1)
                nc_a.activation(KT[:, j, :], KT[:, j, :], ACT.Silu).then_inc(S["k_ready"], 1)
            for j in range(4):
                act.wait_ge(S["qconv"], j + 1)
                nc_a.activation(QT[:, j, :], QT[:, j, :], ACT.Silu).then_inc(S["q_ready"], 1)
            act.wait_ge(S["thr_in"], 1)
            nc_a.activation(t2[:, T:2 * T], t2[:, T:2 * T], ACT.Exp, scale=-1.0
                            ).then_inc(S["thr_ready"], 1)

            act.wait_ge(S["uT_ready"], 1)
            for h in range(MH):
                if h % 2 == 1:
                    i = 4 + h // 2
                    n = W_IN_CHUNKS[i]
                    act.wait_ge(S["w_free"], 16 + 2 * (i + 1))
                    col = n * CH if n < 2 else FW + (n - 6) * CH
                    for b in range(TB):
                        nc_a.copy(A[:, b, col:col + CH], ps[:, 5 + b, :]).then_inc(S["proj_free"], 1)
                act.wait_ge(S["diag_in"], 2 * (h + 1))
                for d in range(2):
                    r = 32 * d + h
                    w = wexp[:, d]
                    mb = ps[:, 2, d * T:(d + 1) * T]
                    for b in range(2):
                        nc_a.activation(w[:, b, :], mb, ACT.Exp, bias=uT[:, b, r:r + 1])
                    off, cols = (2, slice(P, T)) if d == 0 else (3, slice(0, P))
                    nc_a.activation(w[:, off, cols], mb[:, cols], ACT.Exp,
                                    bias=uT[:, off, r:r + 1])
                    for b in range(2):
                        ins = nc_a.activation(w[:, 2 + b, b * P:(b + 1) * P],
                                              w[:, 2 + b, b * P:(b + 1) * P], ACT.Exp)
                    ins.then_inc(S["exp_done"], 1)
            act.wait_ge(S["proj_free"], 25)
            nc_a.activation(A[:, :, FW:D], A[:, :, FW:D], ACT.Sigmoid).then_inc(S["o_sig"], 1)

            for g in range(FG):
                act.wait_ge(S["fn1_done"], g + 1)
                if g >= 2:
                    act.wait_ge(S["fn2_done"], g - 1)
                for b in range(2):
                    src = ps[:, FN_BANKS[g % 2][b], :]
                    nc_a.mul(pts[:, g % 2, b, 0:T], src[:, 0:T], 1.0 / T)
                    nc_a.mul(pts[:, g % 2, b, T:2 * T], src[:, T:2 * T], -1.0 / T
                             ).then_inc(S["fn1_free"], 1)
                if g >= 1:
                    fnet_out(g - 1)
            fnet_out(FG - 1)

            act.wait_ge(S["hsq"], 1)
            nc_a.activation(st[:, 32:40], st[:, 8:16], ACT.Sqrt, bias=eps, scale=1.0 / GW)
            nc_a.activation(st[:, 40:56], st[:, 16:32], ACT.Sqrt, bias=eps, scale=1.0 / DV
                            ).then_inc(S["std"], 1)

            for k in range(KB):
                act.wait_ge(S["yT_psum"], k + 1)
                nc_a.copy(yT[:, k, :], ps[:, k % 4, 0:T]).then_inc(S["yT_ready"], 1)
            for i, dst in enumerate((ga1, sh2)):
                for n in range(4):
                    act.wait_ge(S["bc_psum"], 4 * i + n + 1)
                    nc_a.copy(dst[:, n * CH:(n + 1) * CH], ps[:, 4 + n, :]).then_inc(S["bc_free"], 1)

            act.wait_ge(S["x1_ready"], 8)
            for b in range(TB):
                nc_a.activation(A[:, b, :], B[:, b, :], ACT.Square, accum_out=st[:, b:b + 1]
                                ).then_inc(S["ssq2"], 1)
            act.wait_ge(S["ssq2"], 2)
            nc_a.activation(st[:, 2:4], st[:, 0:2], ACT.Sqrt, bias=eps, scale=1.0 / D
                            ).then_inc(S["std2"], 1)
            for n in range(4):
                act.wait_ge(S["bc_psum"], 12 + n + 1)
                nc_a.copy(ga2[:, n * CH:(n + 1) * CH], ps[:, 4 + n, :]).then_inc(S["bc_free"], 1)
            for i in range(4):
                act.wait_ge(S["keys_psum"], 4 * (i + 1))
                nc_a.copy(keysT[:, 4 * i:4 * i + 4, :],
                          ps[:, i, :].rearrange("p (h n) -> p h n", h=4)).then_inc(S["keys_ready"], 1)
            for k in range(KB):
                act.wait_ge(S["h2T_psum"], k + 1)
                nc_a.copy(h2T[:, k, :], ps[:, 4 + k % 4, 0:T]).then_inc(S["h2T_ready"], 1)
            for n in range(4):
                act.wait_ge(S["w_free"], 40 + 2 * (n + 1))
                for i in range(2):
                    nc_a.copy(qh[:, n % 2, 2 * i:2 * i + 2, :],
                              ps[:, 2 * (n % 2) + i, :].rearrange("p (j t) -> p j t", j=2)
                              ).then_inc(S["q_free"], 1)
                for b in range(TB):
                    act.wait_ge(S["score_psum"], TB * n + b + 1)
                    o = b * 2 * PH * NK + n * CH
                    nc_a.copy(sc[:, o:o + CH], ps[:, 4 + 2 * (n % 2) + b, :]
                              ).then_inc(S["score_ready"], 1)

            with act.Fori(0, TB * PH) as g:
                act.wait_ge(S["dots_ready"], g + 1)
                nc_a.activation(soft[:, bass.ds(g * TOPK, TOPK)], topd[:, bass.ds(g * TOPK, TOPK)],
                                ACT.Exp, accum_out=sums[:, bass.ds(g, 1)])
                nc_a.activation(act_t[:, bass.ds(g * TOPK, TOPK)], dots[:, bass.ds(g * TOPK, TOPK)],
                                ACT.Gelu_apprx_tanh).then_inc(S["gelu_done"], 1)
                act.wait_ge(S["wgt_ready"], g + 1)
                for r in range(TOPK):
                    act.wait_ge(S["pair_free"], g * TOPK + (r + 1))
                    nc_a.activation(diag[:, r % 4, :], ident, ACT.Copy,
                                    scale=wgt[:, bass.ds(g * TOPK + r, 1)]
                                    ).then_inc(S["diag_ready"], 1)
            for b in range(TB):
                act.wait_ge(S["ssq3"], b + 1)
                link(nc_a.activation(A[:, b, :], B[:, b, :], ACT.Square, accum_out=st[:, b:b + 1]))
                nc_a.activation(st[:, 2 + b:3 + b], st[:, b:b + 1], ACT.Sqrt, bias=eps, scale=1.0 / D
                                ).then_inc(S["std3"], 1)

        @block.tensor
        def _(pe):
            mm, tr = nc.tensor.matmul, nc.tensor.transpose
            pe.wait_ge(S["ld_const"], 16)
            pe.wait_ge(S["silu_c"], 1)
            pe.wait_ge(S["ld_rows"], 48)
            tr(ps[:, 7, V_C:V_C + 32], rows[:, 0:P], ident[0:32, 0:32])
            tr(ps[:, 7, V_B:V_B + 32], rows[:, P:2 * P], ident[0:32, 0:32])
            tr(ps[:, 7, V_G:V_G + KB], rows[0:KB, 2 * P:3 * P], ident[0:KB, 0:KB])
            for j in range(8):
                ins = tr(ps[:, 7, V_CONV + 9 * j:V_CONV + 9 * j + 9],
                         conv_rows[:, j * P:(j + 1) * P], ident[0:9, 0:9])
            ins.then_inc(S["vec_psum"], 1)

            pe.wait_ge(S["vec_ready"], 1)
            with pe.Fori(0, 4) as n2:
                for par in range(2):
                    pe.wait_ge(S["moda_free"], n2 * 2 + (par + 1))
                    for kh in range(2):
                        pe.wait_ge(w_ld[kh], n2 * 32 + (16 * par + 16))
                        for k in range(KH):
                            kk = kh * KH + k
                            ins = mm(ps[0:2, par, :], vec[:, kk:32:KB], W[kh][:, k, :],
                                     start=kk == 0, stop=kk == KB - 1)
                        ins.then_inc(S["w_free"], 1)
            pe.wait_ge(S["moda_free"], 2 + 8)
            for j in range(2 * KB):
                ins = tr(ps[:, 7, 2 * j:2 * j + 2], moda[:, j * P:(j + 1) * P], ident[0:2, 0:2])
            ins.then_inc(S["modcol_psum"], 1)

            pe.wait_ge(S["xn_ready"], 4)
            for k in range(KB):
                if k >= 6:
                    pe.wait_ge(S[("ht_act", "ht_dve")[k % 2]], k // 2 - 2)
                for b in range(4):
                    src = (B, A)[b // 2][:, b % 2, k * P:(k + 1) * P]
                    ins = tr(ps[:, k % 6, b * P:(b + 1) * P], src, ident)
                ins.then_inc(S["xT_psum"], 1)
            pe.wait_ge(S["ht_act"], KB // 2)
            pe.wait_ge(S["ht_dve"], KB // 2)

            pe.wait_ge(S["ld_wg"], 64)
            for k in range(KB):
                ins = mm(ps[0:NG, 0, :], wg[:, k, :], H[:, k, :], start=k == 0, stop=k == KB - 1)
            ins.then_inc(S["gates_psum"], 1)

            def reduce_modb(m):
                pe.wait_ge(S["m_free"], 2 * (m + 1))
                if m >= 1:
                    pe.wait_ge(S["modb_free"], m)
                r = 32 * (m // 4)
                mm(ps[r:r + 32, 7, :], ones32, acc[:, m % 2, :], start=True, stop=True
                   ).then_inc(S["modb_red"], 1)

            def project(i, kh, banks):
                n = W_IN_CHUNKS[i]
                pe.wait_ge(w_ld[kh], 16 * (8 + i + 1))
                for j, number in enumerate(banks):
                    if kh == 0 and i < 4 and 4 * i + j + 1 >= 7:
                        pe.wait_ge(S["proj_free"], 4 * i + j + 1 - 6)
                    bank = ps[:, number, :]
                    for k in range(KH):
                        kk = kh * KH + k
                        flags = dict(start=kk == 0, stop=kk == KB - 1)
                        if n == 3:
                            ins = mm(bank, W[kh][:, k, j * P:(j + 1) * P], H[:, kk, :], **flags)
                        elif n == 2:
                            ins = mm(bank[:, 0:T], W[kh][:, k, j * P:(j + 1) * P],
                                     H[:, kk, T:2 * T], **flags)
                        else:
                            b = j if i < 4 else 2 + j
                            ins = mm(bank, H[:, kk, b * P:(b + 1) * P], W[kh][:, k, :], **flags)
                    if j == len(banks) - 1:
                        ins.then_inc(S["w_free"], 1)
                    if (step := 8 * i + 4 * kh + j) in REDUCE_BEHIND and i < 4:
                        reduce_modb(MODB_EARLY + REDUCE_BEHIND.index(step))

            for m in range(MODB_EARLY):
                reduce_modb(m)
            for piece in range(8):
                i, kh = piece // 2, piece % 2
                project(i, kh, [(4 * i + j + 1) % 7 for j in range(4)])

            def columns_of_u():
                pe.wait_ge(S["u_ready"], 1)
                pe.wait_ge(S["thr_ready"], 1)
                for b in range(4):
                    tr(ps[:, 0, b * 40:(b + 1) * 40], gsb[0:40, b * P:(b + 1) * P],
                       ident[0:40, 0:40])
                for b in range(2):
                    ins = tr(ps[:, 0, (4 + b) * 40:(5 + b) * 40], t2[:, T + b * P:T + (b + 1) * P],
                             ident[0:40, 0:40])
                ins.then_inc(S["uT_psum"], 1)
                pe.wait_ge(S["k_ready"], 4)
                pe.wait_ge(S["q_ready"], 4)
                pe.wait_ge(S["ones_v"], 1)
                pe.wait_ge(S["uT_ready"], 1)

            def scores(h):
                if h >= 1:
                    pe.wait_ge(S["p_done"], 2 * h)
                r0 = (h % 2) * DK
                q = QT[r0:r0 + DK, h // 2, :]
                for b in range(4):
                    mm(ps[:, b // 2, (b % 2) * T:(b % 2 + 1) * T],
                       KT[r0:r0 + DK, h // 2, b * P:(b + 1) * P], q, start=True, stop=True)
                for d in range(2):
                    r = 32 * d + h
                    ins = mm(ps[:, 2, d * T:(d + 1) * T],
                             K[0:40, C_ID + r:C_ID + r + 1].to_broadcast([40, P]), negm[:],
                             start=True, stop=True)
                ins.then_inc(S["s_done"], 1)

            def values(h):
                for d in range(2):
                    pe.wait_ge(S["p_done"], 2 * h + d + 1)
                    if h >= 1:
                        pe.wait_ge(S["num_free"], 2 * (h - 1) + d + 1)
                    for j in range(2):
                        blocks = [0, 1] + ([2] if j == 0 else [2, 3]) if d == 0 else \
                            [0, 1] + ([2, 3] if j == 0 else [3])
                        for i, b in enumerate(blocks):
                            ins = mm(ps[:, 3 + d, j * 256:j * 256 + DV + 1],
                                     wexp[:, d, b, j * P:(j + 1) * P], VX[:, b, h, :],
                                     start=i == 0, stop=i == len(blocks) - 1)
                        ins.then_inc(S["num_done"], 1)

            pe.wait_ge(S["proj_free"], 17)
            for h in range(MH):
                if h % 2 == 0:
                    pe.wait_ge(S["proj_free"], 17 + h)
                project(4 + h // 2, h % 2, (5, 6))
                if h == 0:
                    columns_of_u()
                else:
                    values(h - 1)
                scores(h)

            def positions(g):
                if g >= 2:
                    pe.wait_ge(S["fn1_free"], 2 * (g - 1))
                for b in range(2):
                    for t in range(TB):
                        ins = mm(ps[:, FN_BANKS[g % 2][b], :],
                                 A[:, t, g * GW + b * P:g * GW + (b + 1) * P], dft[:, t, :],
                                 start=t == 0, stop=t == TB - 1)
                ins.then_inc(S["fn1_done"], 1)

            def channels(g):
                pe.wait_ge(S["fn1_free"], 2 * (g + 1))
                if g >= 2:
                    pe.wait_ge(S["fn2_free"], 2 * (g - 1))
                for t in range(TB):
                    for i in range(4):
                        part, b = i // 2, i % 2
                        ins = mm(ps[:, (2, 7)[g % 2], t * T:(t + 1) * T],
                                 pts[:, g % 2, b, part * T + t * P:part * T + (t + 1) * P],
                                 dft[:, b, part * T:(part + 1) * T], start=i == 0, stop=i == 3)
                ins.then_inc(S["fn2_done"], 1)

            pe.wait_ge(S["p_done"], 2 * MH)
            values(MH - 1)
            pe.wait_ge(S["proj_free"], 25)
            pe.wait_ge(S["modb_free"], MODB_LATE)
            positions(0)
            for g in range(FG):
                if g + 1 < FG:
                    positions(g + 1)
                channels(g)

            pe.wait_ge(S["y_ready"], 1)
            pe.wait_ge(S["num_free"], 2 * MH)
            for k in range(KB):
                if k >= 4:
                    pe.wait_ge(S["yT_ready"], k - 3)
                for b in range(TB):
                    ins = tr(ps[:, k % 4, b * P:(b + 1) * P], A[:, b, k * P:(k + 1) * P], ident)
                ins.then_inc(S["yT_psum"], 1)

            def spread(r, n):
                mm(ps[:, 4 + n, :], K[:, C_ID + r:C_ID + r + 1].to_broadcast([P, P]),
                   modrow[:, n * CH:(n + 1) * CH], start=True, stop=True
                   ).then_inc(S["bc_psum"], 1)

            for i in range(3):
                for n in range(4):
                    if i >= 1:
                        pe.wait_ge(S["bc_free"], 4 * (i - 1) + n + 1)
                    spread(32 * i, n)
            pe.wait_ge(S["g2_ready"], 4)

            pe.wait_ge(S["yT_ready"], KB)
            with pe.Fori(0, 2) as n2:
                for par in range(2):
                    for b in range(TB):
                        pe.wait_ge(S["out_free"], n2 * 4 + (2 * par + b + 1))
                    for kh in range(2):
                        pe.wait_ge(w_ld[kh], n2 * 32 + 16 * (16 + par + 1))
                        for b in range(TB):
                            for k in range(KH):
                                kk = kh * KH + k
                                ins = mm(ps[:, 2 * par + b, :], yT[:, kk, b * P:(b + 1) * P],
                                         W[kh][:, k, :], start=kk == 0, stop=kk == KB - 1)
                        ins.then_inc(S["w_free"], 1)
                    pe.wait_ge(S["m_free"], n2 * 4 + 2 * (MODB_LATE + par + 1))
                    pe.wait_ge(S["modb_free"], n2 * 2 + (MODB_LATE + par))
                    mm(ps[96:P, 7, :], ones32, acc[:, par, :], start=True, stop=True
                       ).then_inc(S["modb_red"], 1)

            pe.wait_ge(S["ld_keys"], 16)
            pe.wait_ge(S["out_free"], 4 + 8)
            pe.wait_ge(S["modb_free"], MODB)
            for n in range(4):
                spread(96, n)
            for i in range(2 * PH):
                tr(ps[:, i // 4, (i % 4) * P:(i % 4 + 1) * P], keys_raw[:, i, :], ident
                   ).then_inc(S["keys_psum"], 1)
            pe.wait_ge(S["h2_ready"], 2)
            for k in range(KB):
                if k >= 4:
                    pe.wait_ge(S["h2T_ready"], k - 3)
                else:
                    pe.wait_ge(S["bc_free"], 8 + k + 1)
                for b in range(TB):
                    ins = tr(ps[:, 4 + k % 4, b * P:(b + 1) * P], A[:, b, k * P:(k + 1) * P], ident)
                ins.then_inc(S["h2T_psum"], 1)
            pe.wait_ge(S["h2T_ready"], KB)
            pe.wait_ge(S["keys_ready"], 4)

            for n in range(4):
                if n >= 2:
                    pe.wait_ge(S["q_free"], 2 * (n - 1))
                for kh in range(2):
                    pe.wait_ge(w_ld[kh], 16 * (20 + n + 1))
                    for j in range(4):
                        for k in range(KH):
                            kk = kh * KH + k
                            ins = mm(ps[:, 2 * (n % 2) + j // 2, (j % 2) * T:(j % 2 + 1) * T],
                                     W[kh][:, k, j * P:(j + 1) * P], h2T[:, kk, :],
                                     start=kk == 0 and j % 2 == 0, stop=kk == KB - 1,
                                     skip_group_check=True)
                    ins.then_inc(S["w_free"], 1)
                pe.wait_ge(S["q_free"], 2 * (n + 1))
                for b in range(TB):
                    if n >= 2:
                        pe.wait_ge(S["score_ready"], TB * (n - 2) + b + 1)
                    for i in range(4):
                        ins = mm(ps[:, 4 + 2 * (n % 2) + b, i * P:(i + 1) * P],
                                 qh[:, n % 2, i, b * P:(b + 1) * P], keysT[:, 4 * n + i, :],
                                 start=True, stop=True)
                    ins.then_inc(S["score_psum"], 1)
            pe.wait_ge(S["score_ready"], 8)

            for b in range(TB):
                for n in range(4):
                    ins = mm(ps[:, 4 * b + n, :], zeros, K[:, 0:CH], start=True, stop=True)
                if b == 0:
                    ins.then_inc(S["pair_free"], 4)
                quads = PH * TOPK // 4
                with pe.Fori(b * quads, (b + 1) * quads) as q:
                    for s in range(4):
                        pe.wait_ge(S["diag_ready"], q * 4 + (s + 1))
                        pe.wait_ge(v_ld[s], q * 16 + 16)
                        for n in range(4):
                            ins = mm(ps[:, 4 * b + n, :], diag[:, s, :],
                                     ring[:, s, n * CH:(n + 1) * CH],
                                     start=False, stop=False, skip_group_check=True)
                        ins.then_inc(S["pair_free"], 1)

        @block.vector
        def _(dve):
            v = nc.vector
            link = chain(dve, "dve")
            def modb(m):
                for kh in range(2):
                    dve.wait_ge(m_ld[kh], 16 * (m + 1))
                    for k in range(KH):
                        kk = kh * KH + k
                        a = acc[:, m % 2, :]
                        s = vec[:, kk:kk + 1]
                        if kk == 0:
                            ins = v.tensor_scalar(a, W[2 + kh][:, k, :], s, None, ALU.mult)
                        else:
                            ins = v.scalar_tensor_tensor(out=a, in0=W[2 + kh][:, k, :], scalar=s,
                                                         in1=a, op0=ALU.mult, op1=ALU.add)
                        if k == KH - 1:
                            ins.then_inc(S["m_free"], 1)
                            dve.wait_ge(S["m_free"], 2 * m + kh + 1)
                        else:
                            link(ins)

            v.memset(small[:, 0:1], 0.0).then_inc(S["moda_free"], 2)
            dve.wait_ge(S["vec_psum"], 1)
            v.tensor_copy(vec[:], ps[:, 7, 0:V_ALL]).then_inc(S["vec_ready"], 1)
            dve.wait_ge(S["std"], 1)
            v.reciprocal(st[:, 8:12], st[:, 4:8]).then_inc(S["rstd"], 1)
            dve.wait_ge(S["rstd"], 1)
            for i, tile in enumerate((B, A)):
                for b in range(TB):
                    v.tensor_scalar(tile[:, b, :], tile[:, b, :], st[:, 8 + 2 * i + b:9 + 2 * i + b],
                                    None, ALU.mult).then_inc(S["xn_ready"], 1)
            for n in range(8):
                dve.wait_ge(S["w_free"], 2 * n + 2)
                v.tensor_copy(moda[:, n * CH:(n + 1) * CH], ps[0:2, n % 2, :]
                              ).then_inc(S["moda_free"], 1)
                if n in (4, 6):
                    modb((n - 4) // 2)
            dve.wait_ge(S["modcol_psum"], 1)
            dve.wait_ge(S["vec_ready"], 1)
            cols = ps[:, 7, 0:4 * KB].rearrange("p (a k c) -> p a c k", a=2, c=2)
            bias = vec[:, V_B:V_B + 32].rearrange("p (a k) -> p a k", a=2)
            for c_ in range(2):
                v.tensor_tensor(shT[:, c_, :], cols[:, 0, c_, :], bias[:, 0, :], ALU.add)
                link(v.tensor_tensor(gT[:, c_, :], cols[:, 1, c_, :], bias[:, 1, :], ALU.add))
                ins = v.scalar_tensor_tensor(out=gT[:, c_, :], in0=gT[:, c_, :], scalar=1.0,
                                             in1=vec[:, V_G:V_G + KB], op0=ALU.add, op1=ALU.mult)
                if c_ == 1:
                    ins.then_inc(S["mod_ready"], 1)
            dve.wait_ge(S["mod_ready"], 1)
            for k in range(1, KB, 2):
                dve.wait_ge(S["xT_psum"], k + 1)
                for side, c_ in ((0, 1), (1, 0)):
                    w = slice(side * T, (side + 1) * T)
                    ins = v.tensor_scalar(H[:, k, w], ps[:, k % 6, w], gT[:, c_, k:k + 1],
                                          shT[:, c_, k:k + 1], ALU.mult, ALU.add)
                ins.then_inc(S["ht_dve"], 1)

            def modb_out(m):
                dve.wait_ge(S["modb_red"], m + 1)
                r = 32 * (m // 4)
                row = modrow[r:r + 1, (m % 4) * CH:(m % 4 + 1) * CH]
                v.tensor_tensor(row, ps[r:r + 1, 7, :], row, ALU.add).then_inc(S["modb_free"], 1)

            def conv_k(j):
                taps = vec[:, V_CONV + 9 * (4 + j):V_CONV + 9 * (5 + j)]
                link(v.tensor_scalar(KT[:, j, 0:T], kraw[:, j, 0:T], taps[:, 4:5], None, ALU.mult))
                link(v.scalar_tensor_tensor(out=KT[:, j, 1:T], in0=kraw[:, j, 0:T - 1],
                                            scalar=taps[:, 3:4], in1=KT[:, j, 1:T],
                                            op0=ALU.mult, op1=ALU.add))
                link(v.scalar_tensor_tensor(out=KT[:, j, 0:T - 1], in0=kraw[:, j, 1:T],
                                            scalar=taps[:, 5:6], in1=KT[:, j, 0:T - 1],
                                            op0=ALU.mult, op1=ALU.add))
                conv_grid(KT[:, j, T:2 * T], kraw[:, j, T:2 * T], taps, "kconv")

            def conv_grid(dst, src, taps, done):
                link(v.tensor_scalar(dst, src, taps[:, 4:5], None, ALU.mult))
                d = dst.rearrange("p (r w) -> p r w", r=ROWS)
                s = src.rearrange("p (r w) -> p r w", r=ROWS)
                around = [i for i in range(9) if i != 4]
                for i in around:
                    dr, dw = i // 3 - 1, i % 3 - 1
                    r0, r1 = max(0, -dr), ROWS - max(0, dr)
                    c0, c1 = max(0, -dw), GRID_W - max(0, dw)
                    o = d[:, r0:r1, c0:c1]
                    ins = v.scalar_tensor_tensor(out=o, in0=s[:, r0 + dr:r1 + dr, c0 + dw:c1 + dw],
                                                 scalar=taps[:, i:i + 1], in1=o,
                                                 op0=ALU.mult, op1=ALU.add)
                    if i == around[-1]:
                        ins.then_inc(S[done], 1)
                    else:
                        link(ins)

            def gates():
                fg = t1
                dve.wait_ge(S["proj_free"], 1)
                link(v.tensor_copy(fg[:], gsb[64:104, :]))
                link(v.scalar_tensor_tensor(out=t2[:], in0=fg[:], scalar=-1.0, in1=fg[:],
                                            op0=ALU.mult, op1=ALU.max))
                v.tensor_scalar(t1[:], fg[:], 0.0, None, ALU.min).then_inc(S["abs_ready"], 1)

            def scans():
                dve.wait_ge(S["ln_ready"], 1)
                link(v.tensor_tensor(t1[:], t1[:], t2[:], ALU.subtract))
                link(v.memset(t2[:], 0.0))
                one = lambda r, n: K[r:r + MH, C_ONE:C_ONE + 1].to_broadcast([MH, n])
                c_rev = slice(T - 1, None, -1)
                l_rev = slice(2 * T - 1, T - 1, -1)
                link(v.tensor_tensor_scan(t2[0:8, :], one(0, 2 * T), t1[0:8, :], 0.0,
                                          ALU.mult, ALU.add))
                link(v.tensor_tensor_scan(t2[32:40, c_rev], one(32, T), t1[32:40, c_rev], 0.0,
                                          ALU.mult, ALU.add))
                link(v.tensor_tensor_scan(t2[32:40, l_rev], one(32, T), t1[32:40, l_rev],
                                          t2[32:40, 0:1], ALU.mult, ALU.add))
                u = gsb[0:40, :]
                v.tensor_tensor(u, u, t2[:], ALU.subtract).then_inc(S["u_ready"], 1)
                dve.wait_ge(S["u_ready"], 1)
                link(v.memset(t1[:], 0.0))
                link(v.tensor_tensor_scan(t1[0:8, :], u[0:8, :], u[0:8, :], 0.0, ALU.max, ALU.max))
                link(v.tensor_tensor_scan(t1[32:40, c_rev], u[32:40, c_rev], u[32:40, c_rev], 0.0,
                                          ALU.max, ALU.max))
                link(v.tensor_tensor_scan(t1[32:40, l_rev], u[32:40, l_rev], u[32:40, l_rev],
                                          t1[32:40, 0:1], ALU.max, ALU.max))
                v.tensor_scalar(negm[:], t1[:, T:2 * T], -1.0, None, ALU.mult)
                v.tensor_tensor(t2[:, T:2 * T], t2[:, T:2 * T], t1[:, T:2 * T], ALU.add
                                ).then_inc(S["thr_in"], 1)

            dve.wait_ge(S["ld_bm"], 64)
            jobs = {J0: lambda: (gates(), dve.wait_ge(S["proj_free"], 5), conv_k(0))}
            for j in range(1, 4):
                jobs[J0 + j] = lambda j=j: conv_k(j)
            for j in range(4):
                jobs[J0 + 4 + j] = lambda j=j: (dve.wait_ge(S["proj_free"], 9), conv_grid(
                    QT[:, j, :], qraw[:, j, :], vec[:, V_CONV + 9 * j:V_CONV + 9 * (j + 1)], "qconv"))
            for m in range(MODB_EARLY):
                modb_out(m)
            for m in range(MODB_EARLY, MODB_LATE):
                modb(m)
                if m > MODB_EARLY:
                    modb_out(m - 1)
                if m in jobs:
                    jobs[m]()
            modb_out(MODB_LATE - 1)
            scans()
            dve.wait_ge(S["uT_psum"], 1)
            v.tensor_copy(uT[:], ps[:, 0, 0:240].rearrange("p (b r) -> p b r", b=6)
                          ).then_inc(S["uT_ready"], 1)
            dve.wait_ge(S["uT_ready"], 1)

            def diagonals(h):
                dve.wait_ge(S["s_done"], h + 1)
                for d in range(2):
                    for b in range(2):
                        w = wexp[:, d, 2 + b, b * P:(b + 1) * P]
                        ins = v.scalar_tensor_tensor(
                            out=w, in0=ps[:, 2, d * T + b * P:d * T + (b + 1) * P],
                            scalar=uT[:, 2 + b, 32 * d + h:32 * d + h + 1],
                            in1=K[:, C_MASK + d * P:C_MASK + (d + 1) * P], op0=ALU.add, op1=ALU.add)
                    ins.then_inc(S["diag_in"], 1)

            def weigh(h):
                for d in range(2):
                    dve.wait_ge(S["exp_done"], 2 * h + d + 1)
                    w = flat2(wexp[:, d])
                    runs = [(0, 768), (896, 1024)] if d == 0 else [(0, 640), (768, 1024)]
                    parts = []
                    for a, z in runs:
                        parts += [(a, min(z, 512)), (512, z)] if a < 512 < z else [(a, z)]
                    for a, z in parts:
                        bank = a // 512
                        ins = v.scalar_tensor_tensor(
                            out=w[:, a:z], in0=ps[:, bank, a % 512:(z - 1) % 512 + 1],
                            scalar=DK ** -0.5, in1=w[:, a:z], op0=ALU.mult, op1=ALU.mult)
                    ins.then_inc(S["p_done"], 1)

            def flat2(ap):
                return ap.rearrange("p s j -> p (s j)")

            def divide(h):
                for d in range(2):
                    dve.wait_ge(S["num_done"], 4 * h + 2 * d + 2)
                    num = ps[:, 3 + d, :].rearrange("p (j n) -> p j n", j=2)
                    den = num[:, :, DV:DV + 1]
                    r = 32 * d + h
                    q = small[:, 4 + 2 * d:6 + 2 * d].unsqueeze(2)
                    link(v.tensor_copy(q, den))
                    link(v.scalar_tensor_tensor(out=q, in0=q, scalar=-1.0, in1=q,
                                                op0=ALU.mult, op1=ALU.max))
                    link(v.tensor_tensor(q, q, uT[:, 4:6, r:r + 1], ALU.max))
                    link(v.reciprocal(q, q))
                    for j in range(2):
                        o = hm[:, j, h * DV:(h + 1) * DV]
                        s = small[:, 4 + 2 * d + j:5 + 2 * d + j]
                        if d == 0:
                            ins = v.tensor_scalar(o, num[:, j, 0:DV], s, None, ALU.mult)
                        else:
                            ins = v.scalar_tensor_tensor(out=o, in0=num[:, j, 0:DV], scalar=s, in1=o,
                                                         op0=ALU.mult, op1=ALU.add)
                    ins.then_inc(S["num_free"], 1)
                    dve.wait_ge(S["num_free"], 2 * h + d + 1)

            for h in range(MH):
                diagonals(h)
                weigh(h)
                divide(h)

            dve.wait_ge(S["fn2_free"], 2 * FG)
            for b in range(TB):
                sq = tmp[:, 4096 + b * FW:4096 + (b + 1) * FW]
                link(v.tensor_tensor(sq, hm[:, b, :], hm[:, b, :], ALU.mult))
                ins = v.reduce_sum(st[:, 16 + b * MH:16 + (b + 1) * MH],
                                   sq.rearrange("p (h d) -> p h d", h=MH), AX_X)
            ins.then_inc(S["hsq"], 1)
            dve.wait_ge(S["std"], 2)
            link(v.reciprocal(st[:, 32:56], st[:, 32:56]))
            dve.wait_ge(S["o_sig"], 1)
            dve.wait_ge(S["ld_gy"], 32)
            for b in range(TB):
                for g in range(FG):
                    a = A[:, b, g * GW:(g + 1) * GW]
                    v.scalar_tensor_tensor(out=a, in0=a, scalar=st[:, 32 + b * FG + g:33 + b * FG + g],
                                           in1=gy[:, g * GW:(g + 1) * GW], op0=ALU.mult, op1=ALU.mult)
                link(v.tensor_tensor(A[:, b, FW:D], A[:, b, FW:D], gy[:, FW:D], ALU.mult))
                for h in range(MH):
                    a = A[:, b, FW + h * DV:FW + (h + 1) * DV]
                    ins = v.scalar_tensor_tensor(out=a, in0=hm[:, b, h * DV:(h + 1) * DV],
                                                 scalar=st[:, 40 + b * MH + h:41 + b * MH + h], in1=a,
                                                 op0=ALU.mult, op1=ALU.mult)
            ins.then_inc(S["y_ready"], 1)
            v.memset(small[:, 1:2], 0.0).then_inc(S["out_free"], 4)

            dve.wait_ge(S["ld_gffn"], 16)
            for n in range(4):
                dve.wait_ge(S["bc_psum"], 8 + n + 1)
                o = g2[:, n * CH:(n + 1) * CH]
                v.scalar_tensor_tensor(out=o, in0=ps[:, 4 + n, :], scalar=1.0, in1=o, op0=ALU.add,
                                       op1=ALU.mult).then_inc(S["g2_ready"], 1)

            dve.wait_ge(S["ld_x2"], 16)
            dve.wait_ge(S["bc_free"], 8)
            dve.wait_ge(S["g2_ready"], 4)
            for n in range(4):
                modb(MODB_LATE + n)
                if n >= 1:
                    modb_out(MODB_LATE + n - 1)
                dve.wait_ge(S["w_free"], 32 + 2 * n + 2)
                for b in range(TB):
                    o = B[:, b, n * CH:(n + 1) * CH]
                    t = xtmp[:, b * CH:(b + 1) * CH]
                    v.tensor_tensor(t, ps[:, 2 * (n % 2) + b, :], ga1[:, n * CH:(n + 1) * CH],
                                    ALU.mult).then_inc(S["out_free"], 1)
                    dve.wait_ge(S["out_free"], 4 + 2 * n + b + 1)
                    v.tensor_tensor(o, o, t, ALU.add).then_inc(S["x1_ready"], 1)
            modb_out(MODB - 1)

            dve.wait_ge(S["std2"], 1)
            link(v.reciprocal(st[:, 4:6], st[:, 2:4]))
            for b in range(TB):
                link(v.scalar_tensor_tensor(out=A[:, b, :], in0=B[:, b, :], scalar=st[:, 4 + b:5 + b],
                                            in1=g2, op0=ALU.mult, op1=ALU.mult))
                v.tensor_tensor(A[:, b, :], A[:, b, :], sh2, ALU.add).then_inc(S["h2_ready"], 1)

            v.memset(small[:, 3:4], 0.0).then_inc(S["u_free"], 4)
            iota = K[:, C_IOTA:C_IOTA + TOPK]
            steps = dve_chain(dve)

            def pick(g, n):
                step = steps(n)

                def top16(values, indices, src, scratch):
                    dve.nop(nofuse=True)
                    step(v.max(values[:, 0:8], src))
                    dve.nop(nofuse=True)
                    v.max_index(indices[:, 0:8], values[:, 0:8], src)
                    step(v.match_replace(scratch, values[:, 0:8], src, LOWEST))
                    dve.nop(nofuse=True)
                    step(v.max(values[:, 8:16], scratch))
                    dve.nop(nofuse=True)
                    return v.max_index(indices[:, 8:16], values[:, 8:16], scratch)

                grid = [P, TOPK, TOPK]
                sq = lambda t: t.rearrange("p (a c) -> p a c", a=TOPK)
                step(v.tensor_copy(stage, sc[:, bass.ds(g * (2 * NK), 2 * NK)]))
                for p_ in range(2):
                    ins = top16(sv[:, 16 * p_:16 * p_ + 16], siu[:, 16 * p_:16 * p_ + 16],
                                stage[:, p_ * NK:(p_ + 1) * NK], work[:, p_ * NK:(p_ + 1) * NK])
                step(ins)
                v.tensor_copy(si, siu)
                step(v.tensor_tensor(sq(cand), sv[:, 0:16].unsqueeze(2).to_broadcast(grid),
                                     sv[:, 16:32].unsqueeze(1).to_broadcast(grid), ALU.add))
                step(top16(top, pos, cand, work))
                for p_ in range(2):
                    op, k = (ALU.logical_shift_right, 4) if p_ == 0 else (ALU.bitwise_and, 15)
                    step(v.tensor_scalar(half, pos, k, None, op))
                    step(v.tensor_copy(halff, half))
                    step(v.tensor_tensor(sq(work), halff.unsqueeze(2).to_broadcast(grid),
                                         iota.unsqueeze(1).to_broadcast(grid), ALU.is_equal))
                    step(v.tensor_tensor(sq(work), sq(work), si[:, 16 * p_:16 * p_ + 16].unsqueeze(1)
                                         .to_broadcast(grid), ALU.mult))
                    step(v.reduce_sum(sel[:, p_ * 16:(p_ + 1) * 16], sq(work), AX_X))
                step(v.scalar_tensor_tensor(out=eflt, in0=sel[:, 0:16], scalar=float(NK),
                                            in1=sel[:, 16:32], op0=ALU.mult, op1=ALU.add))
                v.tensor_tensor(topd[:, bass.ds(g * TOPK, TOPK)], top,
                                top[:, 0:1].to_broadcast([P, TOPK]), ALU.subtract)
                v.tensor_copy(eidx[:, bass.ds(g * TOPK, TOPK)], eflt).then_inc(S["picked"], 1)
                dve.wait_ge(S["picked"], n + 1)

            def dot(g, b):
                for r in range(TOPK):
                    s = r % 4
                    dve.wait_ge(u_ld[s], g * 64 + 16 * (r // 4 + 1))
                    v.scalar_tensor_tensor(
                        out=ring[:, 4 + s, :], in0=ring[:, 4 + s, :], scalar=1.0, in1=A[:, b, :],
                        op0=ALU.mult, op1=ALU.mult,
                        accum_out=dots[:, bass.ds(g * TOPK + r, 1)]).then_inc(S["u_free"], 1)
                dve.wait_ge(S["u_free"], g * TOPK + (TOPK + 4))
                v.memset(small[:, 2:3], 0.0).then_inc(S["dots_ready"], 1)
                dve.wait_ge(S["gelu_done"], g + 1)
                v.reciprocal(small[:, 1:2], sums[:, bass.ds(g, 1)]).then_inc(S["sums_inv"], 1)
                dve.wait_ge(S["sums_inv"], g + 1)
                v.scalar_tensor_tensor(
                    out=wgt[:, bass.ds(g * TOPK, TOPK)], in0=act_t[:, bass.ds(g * TOPK, TOPK)],
                    scalar=small[:, 1:2], in1=soft[:, bass.ds(g * TOPK, TOPK)],
                    op0=ALU.mult, op1=ALU.mult).then_inc(S["wgt_ready"], 1)

            dve.wait_ge(S["score_ready"], 1)
            pick(0, 0)
            pick(1, 1)
            for b, g0, g1 in ((0, 0, PH), (1, PH, 2 * PH - 2)):
                with dve.Fori(g0, g1) as g:
                    dot(g, b)
                    dve.wait_ge(S["score_ready"], 8)
                    pick(g + 2, g + 2)
            with dve.Fori(2 * PH - 2, 2 * PH) as g:
                dot(g, 1)

            dve.wait_ge(S["ld_gfin"], 16)
            for b in range(TB):
                dve.wait_ge(S["pair_free"], 4 + P * (b + 1))
                for n in range(4):
                    t = ring[:, 4 + b, n * CH:(n + 1) * CH]
                    ins = v.tensor_tensor(t, ps[:, 4 * b + n, :], ga2[:, n * CH:(n + 1) * CH], ALU.mult)
                link(ins)
                v.tensor_tensor(B[:, b, :], B[:, b, :], ring[:, 4 + b, :], ALU.add
                                ).then_inc(S["ssq3"], 1)
                dve.wait_ge(S["std3"], b + 1)
                link(v.reciprocal(st[:, 4 + b:5 + b], st[:, 2 + b:3 + b]))
                v.scalar_tensor_tensor(out=B[:, b, :], in0=B[:, b, :], scalar=st[:, 4 + b:5 + b],
                                       in1=gy[:], op0=ALU.mult, op1=ALU.mult
                                       ).then_inc(S["final_ready"], 1)


INPUTS = ["x", "c", "ctx", "c_ctx", "w_mod", "b_mod", "g_norm_mix", "g_norm_ffn", "w_in", "b_gate",
          "conv_qk", "g_fourier", "g_mlstm", "w_out", "w_query", "sub_keys", "expert_u", "expert_v",
          "g_final"]


def kernel(**inputs):
    from concourse import bacc
    from concourse.bass_utils import run_bass_kernel_spmd

    nc = bacc.Bacc("TRN2", target_bir_lowering=False, num_devices=1)
    arrays = {f"in_{n}": np.ascontiguousarray(inputs[n]) for n in INPUTS}
    arrays["in_consts"] = constants()
    args = [nc.dram_tensor(n, a.shape, mybir.dt.from_np(a.dtype), kind="ExternalInput").ap()
            for n, a in arrays.items()]
    out = nc.dram_tensor("out_x", (1, T, D), F32, kind="ExternalOutput").ap()
    build(nc, *args, out)
    result = run_bass_kernel_spmd(nc, [arrays], core_ids=[0])
    return result.results[0]["out_x"]
```

```python
from contextlib import ExitStack

import numpy as np

import concourse.bass as bass
from concourse import mybir
from concourse.alu_op_type import AluOpType as ALU

F32 = mybir.dt.float32
U32 = mybir.dt.uint32
ACT = mybir.ActivationFunctionType
AX_X = mybir.AxisListType.X

P = 128
D = 2048
KB = D // P
T = 256
TB = T // P
GRID_W = 64
ROWS = T // GRID_W
CH = 512
KH = KB // 2
FW = D // 2
FG = 4
GW = FW // FG
MH = 8
DV = 128
DK = 64
EPS = 1e-6
PH = 8
NK = 128
TOPK = 16
FAR = -1e30
LOWEST = -3e38
FN_BANKS = ((0, 1), (5, 6))
REDUCE_BEHIND = [4, 6, 10, 15, 19, 22, 24, 26, 28, 31]
J0 = 4
SPREAD_ORDER = (0, 2, 1, 3)
LAG = TOPK + TOPK // 2
TAIL_SLOT = 1
TAIL_QUADS = LAG // 4
TAIL_RANK = TB * PH * TOPK - LAG
TAIL_PE = [s for s in range(4) if s != TAIL_SLOT]
Y_BLOCKS = [*range(KB // 2, KB), *range(KB // 2)]
Y_BANKS = (0, 1, 3, 4)
PICK_STEPS = 24

C_ID = 0
C_DFT = C_ID + P
C_MASK = C_DFT + 2 * CH
C_IOTA = C_MASK + 2 * P
C_ONE = C_IOTA + 16
C_EPS = C_ONE + 32
C_ZERO = C_EPS + 1
C_ALL = C_ZERO + P + 15

V_C = 0
V_B = 32
V_G = 64
V_CONV = 80
V_ALL = V_CONV + 72

W_IN_CHUNKS = [3, 2, 4, 5, 0, 1, 6, 7]
GATE_ROWS = [0, 64, 32, 96]
NG = 104
MODB = 16
MODB_EARLY, MODB_LATE = 2, 12


def constants():
    c = np.zeros((P, C_ALL), np.float32)
    c[:, C_ID:C_ID + P] = np.eye(P)
    for b in range(2):
        a = 2 * np.pi * ((np.outer(b * P + np.arange(P), np.arange(T))) % T) / T
        c[:, C_DFT + b * CH:C_DFT + b * CH + T] = np.cos(a)
        c[:, C_DFT + b * CH + T:C_DFT + (b + 1) * CH] = np.sin(a)
    s, j = np.meshgrid(np.arange(P), np.arange(P), indexing="ij")
    c[:, C_MASK:C_MASK + P] = np.where(s <= j, 0.0, FAR)
    c[:, C_MASK + P:C_MASK + 2 * P] = np.where(s >= j, 0.0, FAR)
    c[:, C_IOTA:C_IOTA + 16] = np.arange(16)
    c[:, C_ONE:C_ONE + 32] = 1.0
    c[:, C_EPS] = EPS
    return c


def build(nc, x, c, ctx, c_ctx, w_mod, b_mod, g_norm_mix, g_norm_ffn, w_in, b_gate, conv_qk,
          g_fourier, g_mlstm, w_out, w_query, sub_keys, expert_u, expert_v, g_final, consts, out):
    with ExitStack() as stack:
        def sb(name, shape, dt=F32):
            return stack.enter_context(nc.sbuf_tensor(name, shape, dt))

        def sem(name):
            return stack.enter_context(nc.semaphore(name))

        ps = stack.enter_context(nc.psum_tensor("ps", [P, 8, CH], F32))
        ring = sb("ring", [P, 8, D])
        A = sb("A", [P, TB, D])
        B = sb("B", [P, TB, D])
        H = sb("H", [P, KB, CH])
        KT = sb("KT", [P, 4, 2 * T])
        QT = sb("QT", [P, 4, T])
        VX = sb("VX", [P, 4, MH, DV + 1])
        modrow = sb("modrow", [P, D])
        gy = sb("gy", [P, D])
        K = sb("K", [P, C_ALL])
        wg = sb("wg", [P, KB, NG])
        acc = sb("acc", [P, 2, CH])
        qh = sb("qh", [P, 2, 4, T])
        vec = sb("vec", [P, V_ALL])
        shT = sb("shT", [P, 2, KB])
        gT = sb("gT", [P, 2, KB])
        gsb = sb("gsb", [NG, 2 * T])
        t1 = sb("t1", [40, 2 * T])
        t2 = sb("t2", [40, 2 * T])
        negm = sb("negm", [40, T])
        bg = sb("bg", [NG, 1])
        uT = sb("uT", [P, 6, 40])
        st = sb("st", [P, 64])
        small = sb("small", [P, 16])

        ident = K[:, C_ID:C_ID + P]
        ones32 = K[:, C_ONE:C_ONE + 32]
        eps = K[:, C_EPS:C_EPS + 1]
        zeros = K[:, C_ZERO:C_ZERO + P]
        dft = K[:, C_DFT:C_DFT + 2 * CH].rearrange("p (b n) -> p b n", b=2)
        flat = lambda t: t[:].rearrange("p a b -> p (a b)")
        ringf, Hf, KTf, QTf = flat(ring), flat(H), flat(KT), flat(QT)
        VXf = VX[:].rearrange("p a b c -> p (a b c)")
        W = [ringf[:, i * KH * CH:(i + 1) * KH * CH].rearrange("p (k n) -> p k n", k=KH)
             for i in range(4)]
        rows = flat(acc)[0:32, 0:3 * P]
        moda = VXf[0:2, 0:2 * D]
        gate_cols = KTf[:, 0:KB * 4 * MH].rearrange("p (k n) -> p k n", k=KB)
        conv_rows = QTf[0:9, 0:2 * CH]
        kraw = B[:, 0, :].rearrange("p (j t) -> p j t", j=4)
        qraw = B[:, 1, 0:4 * T].rearrange("p (j t) -> p j t", j=4)
        wexp = B[:, 0, :].rearrange("p (d s j) -> p d s j", d=2, s=4)
        hm = B[:, 1, :].rearrange("p (b n) -> p b n", b=2)
        pts = Hf[:, 6144:8192].rearrange("p (r b n) -> p r b n", r=2, b=2)
        tmp = ringf[:, 0:4 * D]
        yT = Hf[:, 0:4096].rearrange("p (k t) -> p k t", k=KB)
        ga1, sh2 = Hf[:, 4096:6144], Hf[:, 6144:8192]
        ga2 = KTf[:, 0:D]
        g2 = VXf[:, 0:D]
        h2T = yT
        keys_raw = gy[:].rearrange("p (h n) -> p h n", h=2 * PH)
        keysT = modrow[:].rearrange("p (h n) -> p h n", h=2 * PH)
        sc = Hf[:, 4096:8192]
        xtmp = QTf[:, 0:2 * CH]
        stage = QTf[:, 0:2 * NK]
        cand, work = QTf[:, 256:512], QTf[:, 512:768]
        siu, pos, half = (QTf[:, a:z].bitcast(U32) for a, z in ((768, 800), (800, 816), (816, 832)))
        halff, sv, si = QTf[:, 832:848], QTf[:, 848:880], QTf[:, 880:912]
        top, sel, eflt = QTf[:, 912:928], QTf[:, 928:960], QTf[:, 960:976]
        topd, dots, wgt, act_t, soft = (VXf[:, D + 256 * i:D + 256 * (i + 1)] for i in range(5))
        sums = VXf[:, D + 1280:D + 1296]
        eidx = flat(acc)[:, 0:256].bitcast(U32)
        wgf = flat(wg)
        diag = wgf[:, 0:4 * P].rearrange("p (s n) -> p s n", s=4)
        slot_idx = wgf[:, 4 * P:4 * P + 8].bitcast(U32)

        mod_dram = nc.dram_tensor("mod_rows", (4, D), F32, kind="Internal").ap()

        names = """ym_ready wg_ready picked pick_step sums_inv ld_const ld_c ld_rows ld_x ld_ctx ld_wg ld_bg ld_gy ld_bm
        ld_x2 ld_gffn st_mod ld_ga1 ld_sc2 ld_sh2 ld_ga2 ld_keys ld_gfin wg_zero silu_c vec_psum vec_ready moda_free
        modcol_psum mod_ready ssq std rstd xn_ready xT_psum ht_act w_free m_free modb_red
        modb_free proj_free gates_psum abs_ready ln_ready thr_in thr_ready u_ready uT_psum
        uT_ready kconv qconv k_ready q_ready ones_v fn1_done fn1_free fn2_done fn2_free s_done
        diag_in exp_done p_done num_done num_free y_ready yT_psum yT_ready
        g2_ready o_sig hsq out_free x1_ready ssq2 std2 h2_ready h2T_psum h2T_ready keys_psum
        keys_ready q_free score_psum score_ready u_free pair_free dots_ready gelu_done wgt_ready
        diag_ready tail_free copied ssq3 std3 final_ready stored dve act""".split()
        S = {n: sem(n) for n in names}
        w_ld = [sem(f"w_ld{i}") for i in range(2)]
        m_ld = [sem(f"m_ld{i}") for i in range(2)]
        u_ld = [sem(f"u_ld{i}") for i in range(4)]
        v_ld = [sem(f"v_ld{i}") for i in range(4)]

        def chain(engine, name):
            count = [0]

            def link(ins):
                count[0] += 1
                ins.then_inc(S[name], 1)
                engine.wait_ge(S[name], count[0])
            return link

        def dve_chain(engine):
            def steps(n):
                count = [0]

                def step(ins):
                    count[0] += 1
                    assert count[0] <= PICK_STEPS
                    ins.then_inc(S["pick_step"], 1)
                    engine.wait_ge(S["pick_step"], n * PICK_STEPS + count[0])
                return step
            return steps

        block = stack.enter_context(nc.Block())

        @block.sync
        def _(sp):
            sp.dma_start(K[:], consts).then_inc(S["ld_const"], 16)

            def load(piece, src, kh, n0):
                sp.dma_start(W[piece % 2], src[kh * KH * P:(kh + 1) * KH * P, n0].rearrange(
                    "(k p) n -> p k n", p=P)).then_inc(w_ld[piece % 2], 16)

            wm, wi = w_mod[0], w_in[0]
            sp.wait_ge(S["ld_c"], 32)
            sp.wait_ge(S["ld_rows"], 48)
            for kh in range(2):
                load(kh, wm, kh, bass.ds(0, CH))

            def load_moda(n):
                for kh in range(2):
                    sp.wait_ge(S["w_free"], n * 2 + (kh - 1))
                    load(kh, wm, kh, bass.ds(n * CH, CH))

            blocks = [(B, ctx, "ld_ctx", 0), (B, ctx, "ld_ctx", 1), (A, x, "ld_x", 0), (A, x, "ld_x", 1)]
            for n, (tile, src, loaded, b) in enumerate(blocks, 1):
                load_moda(n)
                sp.dma_start(tile[:, b, :], src[0, b * P:(b + 1) * P, :]).then_inc(S[loaded], 16)
            with sp.Fori(5, 8) as n:
                load_moda(n)
            for i, n in enumerate(W_IN_CHUNKS):
                for kh in range(2):
                    sp.wait_ge(S["w_free"], 16 + 2 * i + kh - 1)
                    load(kh, wi, kh, bass.ds(n * CH, CH))
            sp.wait_ge(S["y_ready"], 1)
            for base, src in ((32, w_out[0]), (40, w_query[0])):
                with sp.Fori(0, 4) as n:
                    for kh in range(2):
                        sp.wait_ge(S["w_free"], n * 2 + (base + kh - 1))
                        load(kh, src, kh, bass.ds(n * CH, CH))
            for b in range(TB):
                for half_ in range(2):
                    sp.wait_ge(S["final_ready"], 2 * b + half_ + 1)
                    part = slice(half_ * FW, (half_ + 1) * FW)
                    sp.dma_start(out[0, b * P:(b + 1) * P, part], B[:, b, part]
                                 ).then_inc(S["stored"], 16)
            sp.wait_ge(S["stored"], 16 * 2 * TB)

        @block.gpsimd
        def _(pool):
            nc.gpsimd.memset(wg[:], 0.0).then_inc(S["wg_zero"], 1)
            nc.gpsimd.memset(bg[:], 0.0).then_inc(S["wg_zero"], 1)
            pool.wait_ge(S["wg_zero"], 2)
            pool.wait_ge(S["w_free"], 2)
            gates0 = 8 * CH
            pool.dma_start(gate_cols, w_in[0][:, gates0:gates0 + 4 * MH].rearrange(
                "(k p) n -> p k n", p=P)).then_inc(S["ld_wg"], 16)
            for g, r in enumerate(GATE_ROWS):
                pool.dma_start(bg[r:r + MH, :], b_gate[0:1, g * MH:(g + 1) * MH].rearrange(
                    "a n -> n a")).then_inc(S["ld_bg"], 16)
            for r in range(4):
                pool.dma_start(modrow[32 * r:32 * r + 1, :], b_mod[0:1, (2 + r) * D:(3 + r) * D]
                               ).then_inc(S["ld_bm"], 16)

            pool.wait_ge(S["ld_wg"], 16)
            for g, r in enumerate(GATE_ROWS):
                nc.gpsimd.tensor_copy(wg[:, :, r:r + MH], gate_cols[:, :, g * MH:(g + 1) * MH]
                                      ).then_inc(S["wg_ready"], 1)

            pool.wait_ge(S["w_free"], 14)
            wm = w_mod[0]

            def load(m, kh):
                pool.dma_start(W[2 + kh], wm[kh * KH * P:(kh + 1) * KH * P,
                                             bass.ds(m * CH + 2 * D, CH)].rearrange(
                    "(k p) n -> p k n", p=P)).then_inc(m_ld[kh], 16)
            for kh in range(2):
                load(0, kh)

            def load_from(m0, m1):
                with pool.Fori(m0, m1) as m:
                    for kh in range(2):
                        pool.wait_ge(S["m_free"], m * 2 + (kh - 1))
                        load(m, kh)
            load_from(1, MODB_LATE + 1)
            pool.dma_start(gy[:, 0:FW], g_fourier.to_broadcast([P, FW])).then_inc(S["ld_gy"], 16)
            pool.dma_start(gy[:, FW:D], g_mlstm.to_broadcast([P, FW])).then_inc(S["ld_gy"], 16)
            def spread(r, dst, loaded):
                pool.dma_start(mod_dram[r:r + 1, :], modrow[32 * r:32 * r + 1, :]
                               ).then_inc(S["st_mod"], 16)
                pool.wait_ge(S["st_mod"], 16 * (SPREAD_ORDER.index(r) + 1))
                pool.dma_start(dst, mod_dram[r:r + 1, :].to_broadcast([P, D])
                               ).then_inc(S[loaded], 16)
            pool.wait_ge(S["modb_free"], MODB_LATE)
            pool.wait_ge(S["w_free"], 32)
            spread(0, ga1, "ld_ga1")
            pool.wait_ge(S["num_done"], 4 * MH)
            spread(2, ga2, "ld_sc2")
            pool.dma_start(g2, g_norm_ffn.to_broadcast([P, D])).then_inc(S["ld_gffn"], 16)
            pool.wait_ge(S["fn2_done"], FG)
            spread(1, sh2, "ld_sh2")
            pool.wait_ge(S["y_ready"], 1)
            pool.dma_start(B[:], x[0].rearrange("(b p) d -> p b d", p=P)).then_inc(S["ld_x2"], 16)
            pool.dma_start(keys_raw, sub_keys[0].rearrange("h p n d -> n (h p) d")
                           ).then_inc(S["ld_keys"], 16)
            load_from(MODB_LATE + 1, MODB)
            pool.wait_ge(S["g2_ready"], 1)
            pool.wait_ge(S["modb_free"], MODB)
            spread(3, ga2, "ld_ga2")
            pool.wait_ge(S["keys_psum"], 16)
            pool.dma_start(gy[:], g_final.rearrange("(a d) -> a d", a=1).to_broadcast([P, D])
                           ).then_inc(S["ld_gfin"], 16)

            def gather(table, slot, rank, index, count, loaded):
                nc.gpsimd.tensor_copy(index, eidx[:, bass.ds(rank, 1)]).then_inc(S["copied"], 1)
                pool.wait_ge(S["copied"], count)
                pool.nop(nofuse=True)
                nc.gpsimd.indirect_dma_start(
                    ring[:, slot, :], None, table, bass.IndirectOffsetOnAxis(ap=index, axis=0)
                ).then_inc(loaded, 16)

            def gather_u(rank, s, count):
                pool.wait_ge(S["u_free"], rank + 1)
                gather(expert_u[0], 4 + s, rank, slot_idx[:, s:s + 1], count, u_ld[s])

            def gather_v(rank, s, count):
                pool.wait_ge(S["pair_free"], rank + 1)
                gather(expert_v[0], s, rank, slot_idx[:, 4 + s:5 + s], count, v_ld[s])

            def pairs(q, u_rank, done):
                for s in range(4):
                    gather_u(u_rank + s, s, done + (2 * s + 1))
                    gather_v(u_rank + (s - LAG), s, done + (2 * s + 2))

            ranks = TB * PH * TOPK
            hq = TOPK // 8
            for head, quad, end in ((0, 0, TOPK // 4), (1, TOPK // 4, LAG // 4)):
                pool.wait_ge(S["picked"], head + 1)
                with pool.Fori(quad, end) as q:
                    for s in range(4):
                        gather_u(q * 4 + s, s, q * 4 + (s + 1))
            pool.wait_ge(S["w_free"], 48)
            with pool.Fori(1, TB * PH - 1) as g:
                with pool.Fori(0, hq) as q:
                    pairs(q, g * TOPK + q * 4 + TOPK // 2, g * (2 * TOPK) + q * 8 + (LAG - 2 * TOPK))
                pool.wait_ge(S["picked"], g + 2)
                pool.nop(nofuse=True)
                with pool.Fori(0, hq) as q:
                    pairs(q, g * TOPK + q * 4 + TOPK, g * (2 * TOPK) + q * 8 + (LAG - TOPK))
            with pool.Fori(0, hq) as q:
                pairs(q, q * 4 + (ranks - TOPK // 2), q * 8 + (2 * ranks - LAG - TOPK))
            with pool.Fori(0, TAIL_QUADS) as q:
                for s in range(4):
                    if s == TAIL_SLOT:
                        pool.wait_ge(S["tail_free"], q + 1)
                    else:
                        pool.wait_ge(S["pair_free"], q * 3 + (TAIL_RANK + TAIL_PE.index(s) + 2))
                    gather(expert_v[0], s, q * 4 + (TAIL_RANK + s), slot_idx[:, 4 + s:5 + s],
                           q * 4 + (2 * ranks - LAG + s + 1), v_ld[s])

        @block.scalar
        def _(act):
            link = chain(act, "act")
            nc_a = nc.scalar

            def fnet_out(g):
                act.wait_ge(S["fn2_done"], g + 1)
                for b in range(TB):
                    src = ps[:, (2, 7)[g % 2], b * T:(b + 1) * T]
                    nc_a.copy(A[:, b, g * GW:(g + 1) * GW], src)
                    nc_a.activation(tmp[:, (g * 2 + b) * GW:(g * 2 + b + 1) * GW], src, ACT.Square,
                                    accum_out=st[:, 8 + b * FG + g:9 + b * FG + g]
                                    ).then_inc(S["fn2_free"], 1)

            act.dma_start(rows[0:KB, 0:P], c[0].rearrange("(k p) -> k p", p=P)).then_inc(S["ld_c"], 16)
            act.dma_start(rows[KB:2 * KB, 0:P], c_ctx.rearrange("(k p) -> k p", p=P)
                          ).then_inc(S["ld_c"], 16)
            act.dma_start(rows[0:32, P:2 * P], b_mod[0, 0:2 * D].rearrange("(k p) -> k p", p=P)
                          ).then_inc(S["ld_rows"], 16)
            act.dma_start(rows[0:KB, 2 * P:3 * P], g_norm_mix[0].rearrange("(k p) -> k p", p=P)
                          ).then_inc(S["ld_rows"], 16)
            act.dma_start(conv_rows, conv_qk[0].rearrange("a b n -> (a b) n")
                          ).then_inc(S["ld_rows"], 16)
            act.wait_ge(S["ld_c"], 32)
            nc_a.activation(rows[:, 0:P], rows[:, 0:P], ACT.Silu).then_inc(S["silu_c"], 1)

            act.wait_ge(S["ld_const"], 16)
            for i, (tile, loaded) in enumerate(((B, "ld_ctx"), (A, "ld_x"))):
                act.wait_ge(S[loaded], 32)
                for b in range(TB):
                    o = (2 * i + b) * D
                    nc_a.activation(Hf[:, o:o + D], tile[:, b, :], ACT.Square,
                                    accum_out=st[:, 2 * i + b:2 * i + b + 1]).then_inc(S["ssq"], 1)
            act.wait_ge(S["ssq"], 4)
            nc_a.activation(st[:, 4:8], st[:, 0:4], ACT.Sqrt, bias=eps, scale=1.0 / D
                            ).then_inc(S["std"], 1)

            act.wait_ge(S["mod_ready"], 1)
            for k in range(KB):
                act.wait_ge(S["xT_psum"], k + 1)
                for side, c_ in ((0, 1), (1, 0)):
                    cols = slice(side * T, (side + 1) * T)
                    ins = nc_a.activation(H[:, k, cols], ps[:, k % 6, cols], ACT.Identity,
                                          bias=shT[:, c_, k:k + 1], scale=gT[:, c_, k:k + 1])
                ins.then_inc(S["ht_act"], 1)

            act.wait_ge(S["ld_bg"], 64)
            act.wait_ge(S["gates_psum"], 1)
            nc_a.activation(gsb[:], ps[0:NG, 0, :], ACT.Identity, bias=bg[:]
                            ).then_inc(S["proj_free"], 1)
            group = 1
            for i, n in enumerate(W_IN_CHUNKS[:4]):
                act.wait_ge(S["w_free"], 16 + 2 * (i + 1))
                for j in range(4):
                    bank = ps[:, group % 7, :]
                    if n == 3:
                        dst, src = kraw[:, j, :], bank
                    elif n == 2:
                        dst, src = qraw[:, j, :], bank[:, 0:T]
                    else:
                        h0 = (n - 4) * 4
                        dst = VX[:, j, h0:h0 + 4, 0:DV]
                        src = bank.rearrange("p (h d) -> p h d", h=4)
                    nc_a.copy(dst, src).then_inc(S["proj_free"], 1)
                    group += 1
                if n == 2:
                    act.wait_ge(S["abs_ready"], 1)
                    link(nc_a.activation(t2[:], t2[:], ACT.Exp, scale=-1.0))
                    nc_a.activation(t2[:], t2[:], ACT.Ln, bias=K[0:40, C_ONE:C_ONE + 1]
                                    ).then_inc(S["ln_ready"], 1)
            for b in range(4):
                ins = nc_a.activation(VX[:, b, :, DV:DV + 1], K[:, C_ONE:C_ONE + MH].unsqueeze(2),
                                      ACT.Copy)
            ins.then_inc(S["ones_v"], 1)

            for j in range(4):
                act.wait_ge(S["kconv"], j + 1)
                nc_a.activation(KT[:, j, :], KT[:, j, :], ACT.Silu).then_inc(S["k_ready"], 1)
            for j in range(4):
                act.wait_ge(S["qconv"], j + 1)
                nc_a.activation(QT[:, j, :], QT[:, j, :], ACT.Silu).then_inc(S["q_ready"], 1)
            act.wait_ge(S["thr_in"], 1)
            nc_a.activation(t2[:, T:2 * T], t2[:, T:2 * T], ACT.Exp, scale=-1.0
                            ).then_inc(S["thr_ready"], 1)

            act.wait_ge(S["uT_ready"], 1)
            for h in range(MH):
                if h % 2 == 1:
                    i = 4 + h // 2
                    n = W_IN_CHUNKS[i]
                    act.wait_ge(S["w_free"], 16 + 2 * (i + 1))
                    col = n * CH if n < 2 else FW + (n - 6) * CH
                    for b in range(TB):
                        nc_a.copy(A[:, b, col:col + CH], ps[:, 5 + b, :]).then_inc(S["proj_free"], 1)
                act.wait_ge(S["diag_in"], 2 * (h + 1))
                for d in range(2):
                    r = 32 * d + h
                    w = wexp[:, d]
                    mb = ps[:, 2, d * T:(d + 1) * T]
                    for b in range(2):
                        nc_a.activation(w[:, b, :], mb, ACT.Exp, bias=uT[:, b, r:r + 1])
                    off, cols = (2, slice(P, T)) if d == 0 else (3, slice(0, P))
                    nc_a.activation(w[:, off, cols], mb[:, cols], ACT.Exp,
                                    bias=uT[:, off, r:r + 1])
                    for b in range(2):
                        ins = nc_a.activation(w[:, 2 + b, b * P:(b + 1) * P],
                                              w[:, 2 + b, b * P:(b + 1) * P], ACT.Exp)
                    ins.then_inc(S["exp_done"], 1)
            act.wait_ge(S["proj_free"], 25)
            nc_a.activation(A[:, :, FW:D], A[:, :, FW:D], ACT.Sigmoid).then_inc(S["o_sig"], 1)

            for g in range(FG):
                act.wait_ge(S["fn1_done"], g + 1)
                if g >= 2:
                    act.wait_ge(S["fn2_done"], g - 1)
                for b in range(2):
                    src = ps[:, FN_BANKS[g % 2][b], :]
                    nc_a.mul(pts[:, g % 2, b, 0:T], src[:, 0:T], 1.0 / T)
                    nc_a.mul(pts[:, g % 2, b, T:2 * T], src[:, T:2 * T], -1.0 / T
                             ).then_inc(S["fn1_free"], 1)
                if g >= 1:
                    fnet_out(g - 1)
            act.wait_ge(S["hsq"], 1)
            nc_a.activation(st[:, 40:56], st[:, 16:32], ACT.Sqrt, bias=eps, scale=1.0 / DV
                            ).then_inc(S["std"], 1)
            fnet_out(FG - 1)
            act.wait_ge(S["fn2_free"], 2 * FG)
            nc_a.activation(st[:, 32:40], st[:, 8:16], ACT.Sqrt, bias=eps, scale=1.0 / GW
                            ).then_inc(S["std"], 1)

            for i, k in enumerate(Y_BLOCKS):
                act.wait_ge(S["yT_psum"], i + 1)
                nc_a.copy(yT[:, k, :], ps[:, Y_BANKS[i % 4], 0:T]).then_inc(S["yT_ready"], 1)
            for n in range(4):
                for b in range(TB):
                    act.wait_ge(S["x1_ready"], TB * n + b + 1)
                    cols = slice(n * CH, (n + 1) * CH)
                    nc_a.activation(A[:, b, cols], B[:, b, cols], ACT.Square,
                                    accum_out=st[:, 16 + 4 * b + n:17 + 4 * b + n]
                                    ).then_inc(S["ssq2"], 1)
            act.wait_ge(S["ssq2"], 8)
            for b in range(TB):
                ins = nc_a.activation(st[:, 48 + 4 * b:52 + 4 * b], st[:, 16 + 4 * b:20 + 4 * b],
                                      ACT.Identity, scale=1.0 / D, accum_out=st[:, b:b + 1])
            link(ins)
            nc_a.activation(st[:, 2:4], st[:, 0:2], ACT.Sqrt, bias=eps).then_inc(S["std2"], 1)
            act.wait_ge(S["st_mod"], 16 * 4)
            for i in range(4):
                act.wait_ge(S["keys_psum"], 4 * (i + 1))
                nc_a.copy(keysT[:, 4 * i:4 * i + 4, :],
                          ps[:, i, :].rearrange("p (h n) -> p h n", h=4)).then_inc(S["keys_ready"], 1)
            for k in range(KB):
                act.wait_ge(S["h2T_psum"], k + 1)
                nc_a.copy(h2T[:, k, :], ps[:, 4 + k % 4, 0:T]).then_inc(S["h2T_ready"], 1)
            for n in range(4):
                act.wait_ge(S["w_free"], 40 + 2 * (n + 1))
                for i in range(2):
                    nc_a.copy(qh[:, n % 2, 2 * i:2 * i + 2, :],
                              ps[:, 2 * (n % 2) + i, :].rearrange("p (j t) -> p j t", j=2)
                              ).then_inc(S["q_free"], 1)
                for b in range(TB):
                    act.wait_ge(S["score_psum"], TB * n + b + 1)
                    o = b * 2 * PH * NK + n * CH
                    nc_a.copy(sc[:, o:o + CH], ps[:, 4 + 2 * (n % 2) + b, :]
                              ).then_inc(S["score_ready"], 1)

            def head(g, nth):
                act.wait_ge(S["dots_ready"], nth)
                nc_a.activation(soft[:, bass.ds(g * TOPK, TOPK)], topd[:, bass.ds(g * TOPK, TOPK)],
                                ACT.Exp, accum_out=sums[:, bass.ds(g, 1)])
                nc_a.activation(act_t[:, bass.ds(g * TOPK, TOPK)], dots[:, bass.ds(g * TOPK, TOPK)],
                                ACT.Gelu_apprx_tanh).then_inc(S["gelu_done"], 1)
                act.wait_ge(S["wgt_ready"], nth)

            def diagonal(rank, slot):
                nc_a.activation(diag[:, slot, :], ident, ACT.Copy, scale=wgt[:, bass.ds(rank, 1)]
                                ).then_inc(S["diag_ready"], 1)

            with act.Fori(0, TAIL_RANK // TOPK) as g:
                head(g, g + 1)
                for r in range(TOPK):
                    act.wait_ge(S["pair_free"], g * TOPK + (r + 1))
                    diagonal(g * TOPK + r, r % 4)
            n = 0
            for g in range(TAIL_RANK // TOPK, TB * PH):
                head(g, g + 1)
                for rank in range(g * TOPK, (g + 1) * TOPK):
                    if rank < TAIL_RANK:
                        act.wait_ge(S["pair_free"], rank + 1)
                        diagonal(rank, rank % 4)
                    elif rank % 4 != TAIL_SLOT:
                        act.wait_ge(S["pair_free"], TAIL_RANK + n + 2)
                        diagonal(rank, rank % 4)
                        n += 1
            for b in range(TB):
                for half_ in range(2):
                    act.wait_ge(S["ssq3"], 2 * b + half_ + 1)
                    part = slice(half_ * FW, (half_ + 1) * FW)
                    ins = nc_a.activation(A[:, b, part], B[:, b, part], ACT.Square,
                                          accum_out=st[:, 8 * half_:8 * half_ + 1])
                link(ins)
                link(nc_a.activation(st[:, 16:17], st[:, 0:1], ACT.Identity, bias=eps, scale=1.0 / D))
                nc_a.activation(st[:, 2 + b:3 + b], st[:, 8:9], ACT.Sqrt, bias=st[:, 16:17],
                                scale=1.0 / D
                                ).then_inc(S["std3"], 1)

        @block.tensor
        def _(pe):
            mm, tr = nc.tensor.matmul, nc.tensor.transpose
            pe.wait_ge(S["ld_const"], 16)
            pe.wait_ge(S["silu_c"], 1)
            pe.wait_ge(S["ld_rows"], 48)
            tr(ps[:, 7, V_C:V_C + 32], rows[:, 0:P], ident[0:32, 0:32])
            tr(ps[:, 7, V_B:V_B + 32], rows[:, P:2 * P], ident[0:32, 0:32])
            tr(ps[:, 7, V_G:V_G + KB], rows[0:KB, 2 * P:3 * P], ident[0:KB, 0:KB])
            for j in range(8):
                ins = tr(ps[:, 7, V_CONV + 9 * j:V_CONV + 9 * j + 9],
                         conv_rows[:, j * P:(j + 1) * P], ident[0:9, 0:9])
            ins.then_inc(S["vec_psum"], 1)

            pe.wait_ge(S["vec_ready"], 1)
            with pe.Fori(0, 4) as n2:
                for par in range(2):
                    pe.wait_ge(S["moda_free"], n2 * 2 + (par + 1))
                    for kh in range(2):
                        pe.wait_ge(w_ld[kh], n2 * 32 + (16 * par + 16))
                        for k in range(KH):
                            kk = kh * KH + k
                            ins = mm(ps[0:2, par, :], vec[:, kk:32:KB], W[kh][:, k, :],
                                     start=kk == 0, stop=kk == KB - 1)
                        ins.then_inc(S["w_free"], 1)
            pe.wait_ge(S["moda_free"], 2 + 8)
            for j in range(2 * KB):
                ins = tr(ps[:, 7, 2 * j:2 * j + 2], moda[:, j * P:(j + 1) * P], ident[0:2, 0:2])
            ins.then_inc(S["modcol_psum"], 1)

            pe.wait_ge(S["xn_ready"], 4)
            for k in range(KB):
                if k >= 6:
                    pe.wait_ge(S["ht_act"], k - 5)
                for b in range(4):
                    src = (B, A)[b // 2][:, b % 2, k * P:(k + 1) * P]
                    ins = tr(ps[:, k % 6, b * P:(b + 1) * P], src, ident)
                ins.then_inc(S["xT_psum"], 1)
            pe.wait_ge(S["ht_act"], KB)

            pe.wait_ge(S["wg_ready"], 4)
            for k in range(KB):
                ins = mm(ps[0:NG, 0, :], wg[:, k, :], H[:, k, :], start=k == 0, stop=k == KB - 1)
            ins.then_inc(S["gates_psum"], 1)

            def reduce_modb(m):
                pe.wait_ge(S["m_free"], 2 * (m + 1))
                if m >= 1:
                    pe.wait_ge(S["modb_free"], m)
                r = 32 * (m // 4)
                mm(ps[r:r + 32, 7, :], ones32, acc[:, m % 2, :], start=True, stop=True
                   ).then_inc(S["modb_red"], 1)

            def project(i, kh, banks):
                n = W_IN_CHUNKS[i]
                pe.wait_ge(w_ld[kh], 16 * (8 + i + 1))
                for j, number in enumerate(banks):
                    if kh == 0 and i < 4 and 4 * i + j + 1 >= 7:
                        pe.wait_ge(S["proj_free"], 4 * i + j + 1 - 6)
                    bank = ps[:, number, :]
                    for k in range(KH):
                        kk = kh * KH + k
                        flags = dict(start=kk == 0, stop=kk == KB - 1)
                        if n == 3:
                            ins = mm(bank, W[kh][:, k, j * P:(j + 1) * P], H[:, kk, :], **flags)
                        elif n == 2:
                            ins = mm(bank[:, 0:T], W[kh][:, k, j * P:(j + 1) * P],
                                     H[:, kk, T:2 * T], **flags)
                        else:
                            b = j if i < 4 else 2 + j
                            ins = mm(bank, H[:, kk, b * P:(b + 1) * P], W[kh][:, k, :], **flags)
                    if j == len(banks) - 1:
                        ins.then_inc(S["w_free"], 1)
                    if (step := 8 * i + 4 * kh + j) in REDUCE_BEHIND and i < 4:
                        reduce_modb(MODB_EARLY + REDUCE_BEHIND.index(step))

            for m in range(MODB_EARLY):
                reduce_modb(m)
            for piece in range(8):
                i, kh = piece // 2, piece % 2
                project(i, kh, [(4 * i + j + 1) % 7 for j in range(4)])

            def columns_of_u():
                pe.wait_ge(S["u_ready"], 1)
                pe.wait_ge(S["thr_ready"], 1)
                for b in range(4):
                    tr(ps[:, 0, b * 40:(b + 1) * 40], gsb[0:40, b * P:(b + 1) * P],
                       ident[0:40, 0:40])
                for b in range(2):
                    ins = tr(ps[:, 0, (4 + b) * 40:(5 + b) * 40], t2[:, T + b * P:T + (b + 1) * P],
                             ident[0:40, 0:40])
                ins.then_inc(S["uT_psum"], 1)
                pe.wait_ge(S["k_ready"], 4)
                pe.wait_ge(S["q_ready"], 4)
                pe.wait_ge(S["ones_v"], 1)
                pe.wait_ge(S["uT_ready"], 1)

            def scores(h):
                if h >= 1:
                    pe.wait_ge(S["p_done"], 2 * h)
                r0 = (h % 2) * DK
                q = QT[r0:r0 + DK, h // 2, :]
                for b in range(4):
                    mm(ps[:, b // 2, (b % 2) * T:(b % 2 + 1) * T],
                       KT[r0:r0 + DK, h // 2, b * P:(b + 1) * P], q, start=True, stop=True)
                for d in range(2):
                    r = 32 * d + h
                    ins = mm(ps[:, 2, d * T:(d + 1) * T],
                             K[0:40, C_ID + r:C_ID + r + 1].to_broadcast([40, P]), negm[:],
                             start=True, stop=True)
                ins.then_inc(S["s_done"], 1)

            def values(h):
                for d in range(2):
                    pe.wait_ge(S["p_done"], 2 * h + d + 1)
                    if h >= 1:
                        pe.wait_ge(S["num_free"], 2 * (h - 1) + d + 1)
                    for j in range(2):
                        blocks = [0, 1] + ([2] if j == 0 else [2, 3]) if d == 0 else \
                            [0, 1] + ([2, 3] if j == 0 else [3])
                        for i, b in enumerate(blocks):
                            ins = mm(ps[:, 3 + d, j * 256:j * 256 + DV + 1],
                                     wexp[:, d, b, j * P:(j + 1) * P], VX[:, b, h, :],
                                     start=i == 0, stop=i == len(blocks) - 1)
                        ins.then_inc(S["num_done"], 1)

            pe.wait_ge(S["proj_free"], 17)
            for h in range(MH):
                if h % 2 == 0:
                    pe.wait_ge(S["proj_free"], 17 + h)
                project(4 + h // 2, h % 2, (5, 6))
                if h == 0:
                    columns_of_u()
                else:
                    values(h - 1)
                scores(h)

            def positions(g):
                if g >= 2:
                    pe.wait_ge(S["fn1_free"], 2 * (g - 1))
                for b in range(2):
                    for t in range(TB):
                        ins = mm(ps[:, FN_BANKS[g % 2][b], :],
                                 A[:, t, g * GW + b * P:g * GW + (b + 1) * P], dft[:, t, :],
                                 start=t == 0, stop=t == TB - 1)
                ins.then_inc(S["fn1_done"], 1)

            def channels(g):
                pe.wait_ge(S["fn1_free"], 2 * (g + 1))
                if g >= 2:
                    pe.wait_ge(S["fn2_free"], 2 * (g - 1))
                for t in range(TB):
                    for i in range(4):
                        part, b = i // 2, i % 2
                        ins = mm(ps[:, (2, 7)[g % 2], t * T:(t + 1) * T],
                                 pts[:, g % 2, b, part * T + t * P:part * T + (t + 1) * P],
                                 dft[:, b, part * T:(part + 1) * T], start=i == 0, stop=i == 3)
                ins.then_inc(S["fn2_done"], 1)

            pe.wait_ge(S["p_done"], 2 * MH)
            values(MH - 1)
            pe.wait_ge(S["proj_free"], 25)
            pe.wait_ge(S["modb_free"], MODB_LATE)
            positions(0)
            for g in range(FG):
                if g + 1 < FG:
                    positions(g + 1)
                channels(g)

            pe.wait_ge(S["ym_ready"], 1)
            pe.wait_ge(S["num_free"], 2 * MH)
            for i, k in enumerate(Y_BLOCKS):
                if i == KB // 2:
                    pe.wait_ge(S["y_ready"], 1)
                if i >= 4:
                    pe.wait_ge(S["yT_ready"], i - 3)
                for b in range(TB):
                    ins = tr(ps[:, Y_BANKS[i % 4], b * P:(b + 1) * P], A[:, b, k * P:(k + 1) * P],
                             ident)
                ins.then_inc(S["yT_psum"], 1)
            pe.wait_ge(S["yT_ready"], KB)

            with pe.Fori(0, 2) as n2:
                for par in range(2):
                    for b in range(TB):
                        pe.wait_ge(S["out_free"], n2 * 4 + (2 * par + b + 1))
                    for kh in range(2):
                        pe.wait_ge(w_ld[kh], n2 * 32 + 16 * (16 + par + 1))
                        for b in range(TB):
                            for k in range(KH):
                                kk = kh * KH + k
                                ins = mm(ps[:, 2 * par + b, :], yT[:, kk, b * P:(b + 1) * P],
                                         W[kh][:, k, :], start=kk == 0, stop=kk == KB - 1)
                        ins.then_inc(S["w_free"], 1)
                    pe.wait_ge(S["m_free"], n2 * 4 + 2 * (MODB_LATE + par + 1))
                    pe.wait_ge(S["modb_free"], n2 * 2 + (MODB_LATE + par))
                    mm(ps[96:P, 7, :], ones32, acc[:, par, :], start=True, stop=True
                       ).then_inc(S["modb_red"], 1)

            pe.wait_ge(S["ld_keys"], 16)
            pe.wait_ge(S["out_free"], 4 + 8)
            pe.wait_ge(S["modb_free"], MODB)
            for i in range(2 * PH):
                tr(ps[:, i // 4, (i % 4) * P:(i % 4 + 1) * P], keys_raw[:, i, :], ident
                   ).then_inc(S["keys_psum"], 1)
            for k in range(KB):
                if k % (KB // 2) == 0:
                    pe.wait_ge(S["h2_ready"], TB * (k // (KB // 2) + 1))
                if k >= 4:
                    pe.wait_ge(S["h2T_ready"], k - 3)
                for b in range(TB):
                    ins = tr(ps[:, 4 + k % 4, b * P:(b + 1) * P], A[:, b, k * P:(k + 1) * P], ident)
                ins.then_inc(S["h2T_psum"], 1)
            pe.wait_ge(S["h2T_ready"], KB)
            pe.wait_ge(S["keys_ready"], 4)

            for n in range(4):
                if n >= 2:
                    pe.wait_ge(S["q_free"], 2 * (n - 1))
                for kh in range(2):
                    pe.wait_ge(w_ld[kh], 16 * (20 + n + 1))
                    for j in range(4):
                        for k in range(KH):
                            kk = kh * KH + k
                            ins = mm(ps[:, 2 * (n % 2) + j // 2, (j % 2) * T:(j % 2 + 1) * T],
                                     W[kh][:, k, j * P:(j + 1) * P], h2T[:, kk, :],
                                     start=kk == 0 and j % 2 == 0, stop=kk == KB - 1,
                                     skip_group_check=True)
                    ins.then_inc(S["w_free"], 1)
                pe.wait_ge(S["q_free"], 2 * (n + 1))
                for b in range(TB):
                    if n >= 2:
                        pe.wait_ge(S["score_ready"], TB * (n - 2) + b + 1)
                    for i in range(4):
                        ins = mm(ps[:, 4 + 2 * (n % 2) + b, i * P:(i + 1) * P],
                                 qh[:, n % 2, i, b * P:(b + 1) * P], keysT[:, 4 * n + i, :],
                                 start=True, stop=True)
                    ins.then_inc(S["score_psum"], 1)
            pe.wait_ge(S["score_ready"], 8)

            for b in range(TB):
                for n in range(4):
                    ins = mm(ps[:, 4 * b + n, :], zeros, K[:, 0:CH], start=True, stop=True)
                if b == 0:
                    ins.then_inc(S["pair_free"], 4)

                def rank_of_v(s, diags, loads):
                    pe.wait_ge(S["diag_ready"], diags)
                    pe.wait_ge(v_ld[s], loads)
                    for n in range(4):
                        ins = mm(ps[:, 4 * b + n, :], diag[:, s, :],
                                 ring[:, s, n * CH:(n + 1) * CH],
                                 start=False, stop=False, skip_group_check=True)
                    ins.then_inc(S["pair_free"], 1)

                quads = PH * TOPK // 4
                with pe.Fori(b * quads, quads if b == 0 else TAIL_RANK // 4) as q:
                    for s in range(4):
                        rank_of_v(s, q * 4 + (s + 1), q * 16 + 16)
            with pe.Fori(0, TAIL_QUADS) as q:
                for i, s in enumerate(TAIL_PE):
                    rank_of_v(s, q * 3 + (TAIL_RANK + i + 1), q * 16 + 16 * (TAIL_RANK // 4 + 1))

        @block.vector
        def _(dve):
            v = nc.vector
            link = chain(dve, "dve")
            def modb(m):
                for kh in range(2):
                    dve.wait_ge(m_ld[kh], 16 * (m + 1))
                    for k in range(KH):
                        kk = kh * KH + k
                        a = acc[:, m % 2, :]
                        s = vec[:, kk:kk + 1]
                        if kk == 0:
                            ins = v.tensor_scalar(a, W[2 + kh][:, k, :], s, None, ALU.mult)
                        else:
                            ins = v.scalar_tensor_tensor(out=a, in0=W[2 + kh][:, k, :], scalar=s,
                                                         in1=a, op0=ALU.mult, op1=ALU.add)
                        if k == KH - 1:
                            ins.then_inc(S["m_free"], 1)
                            dve.wait_ge(S["m_free"], 2 * m + kh + 1)
                        else:
                            link(ins)

            v.memset(small[:, 0:1], 0.0).then_inc(S["moda_free"], 2)
            dve.wait_ge(S["vec_psum"], 1)
            v.tensor_copy(vec[:], ps[:, 7, 0:V_ALL]).then_inc(S["vec_ready"], 1)
            def norm_tokens():
                dve.wait_ge(S["std"], 1)
                v.reciprocal(st[:, 8:12], st[:, 4:8]).then_inc(S["rstd"], 1)
                dve.wait_ge(S["rstd"], 1)
                for i, tile in enumerate((B, A)):
                    for b in range(TB):
                        v.tensor_scalar(tile[:, b, :], tile[:, b, :], st[:, 8 + 2 * i + b:9 + 2 * i + b],
                                        None, ALU.mult).then_inc(S["xn_ready"], 1)

            for n in range(8):
                dve.wait_ge(S["w_free"], 2 * n + 2)
                v.tensor_copy(moda[:, n * CH:(n + 1) * CH], ps[0:2, n % 2, :]
                              ).then_inc(S["moda_free"], 1)
                if n == 4:
                    norm_tokens()
            dve.wait_ge(S["modcol_psum"], 1)
            dve.wait_ge(S["vec_ready"], 1)
            cols = ps[:, 7, 0:4 * KB].rearrange("p (a k c) -> p a c k", a=2, c=2)
            bias = vec[:, V_B:V_B + 32].rearrange("p (a k) -> p a k", a=2)
            for c_ in range(2):
                v.tensor_tensor(shT[:, c_, :], cols[:, 0, c_, :], bias[:, 0, :], ALU.add)
                link(v.tensor_tensor(gT[:, c_, :], cols[:, 1, c_, :], bias[:, 1, :], ALU.add))
                ins = v.scalar_tensor_tensor(out=gT[:, c_, :], in0=gT[:, c_, :], scalar=1.0,
                                             in1=vec[:, V_G:V_G + KB], op0=ALU.add, op1=ALU.mult)
                if c_ == 1:
                    ins.then_inc(S["mod_ready"], 1)

            def modb_out(m):
                dve.wait_ge(S["modb_red"], m + 1)
                r = 32 * (m // 4)
                row = modrow[r:r + 1, (m % 4) * CH:(m % 4 + 1) * CH]
                v.tensor_tensor(row, ps[r:r + 1, 7, :], row, ALU.add).then_inc(S["modb_free"], 1)

            def conv_k(j):
                taps = vec[:, V_CONV + 9 * (4 + j):V_CONV + 9 * (5 + j)]
                link(v.tensor_scalar(KT[:, j, 0:T], kraw[:, j, 0:T], taps[:, 4:5], None, ALU.mult))
                link(v.scalar_tensor_tensor(out=KT[:, j, 1:T], in0=kraw[:, j, 0:T - 1],
                                            scalar=taps[:, 3:4], in1=KT[:, j, 1:T],
                                            op0=ALU.mult, op1=ALU.add))
                link(v.scalar_tensor_tensor(out=KT[:, j, 0:T - 1], in0=kraw[:, j, 1:T],
                                            scalar=taps[:, 5:6], in1=KT[:, j, 0:T - 1],
                                            op0=ALU.mult, op1=ALU.add))
                conv_grid(KT[:, j, T:2 * T], kraw[:, j, T:2 * T], taps, "kconv")

            def conv_grid(dst, src, taps, done):
                link(v.tensor_scalar(dst, src, taps[:, 4:5], None, ALU.mult))
                d = dst.rearrange("p (r w) -> p r w", r=ROWS)
                s = src.rearrange("p (r w) -> p r w", r=ROWS)
                around = [i for i in range(9) if i != 4]
                for i in around:
                    dr, dw = i // 3 - 1, i % 3 - 1
                    r0, r1 = max(0, -dr), ROWS - max(0, dr)
                    c0, c1 = max(0, -dw), GRID_W - max(0, dw)
                    o = d[:, r0:r1, c0:c1]
                    ins = v.scalar_tensor_tensor(out=o, in0=s[:, r0 + dr:r1 + dr, c0 + dw:c1 + dw],
                                                 scalar=taps[:, i:i + 1], in1=o,
                                                 op0=ALU.mult, op1=ALU.add)
                    if i == around[-1]:
                        ins.then_inc(S[done], 1)
                    else:
                        link(ins)

            def gates():
                fg = t1
                dve.wait_ge(S["proj_free"], 1)
                link(v.tensor_copy(fg[:], gsb[64:104, :]))
                link(v.scalar_tensor_tensor(out=t2[:], in0=fg[:], scalar=-1.0, in1=fg[:],
                                            op0=ALU.mult, op1=ALU.max))
                v.tensor_scalar(t1[:], fg[:], 0.0, None, ALU.min).then_inc(S["abs_ready"], 1)

            def scans():
                dve.wait_ge(S["ln_ready"], 1)
                link(v.tensor_tensor(t1[:], t1[:], t2[:], ALU.subtract))
                link(v.memset(t2[:], 0.0))
                one = lambda r, n: K[r:r + MH, C_ONE:C_ONE + 1].to_broadcast([MH, n])
                c_rev = slice(T - 1, None, -1)
                l_rev = slice(2 * T - 1, T - 1, -1)
                link(v.tensor_tensor_scan(t2[0:8, :], one(0, 2 * T), t1[0:8, :], 0.0,
                                          ALU.mult, ALU.add))
                link(v.tensor_tensor_scan(t2[32:40, c_rev], one(32, T), t1[32:40, c_rev], 0.0,
                                          ALU.mult, ALU.add))
                link(v.tensor_tensor_scan(t2[32:40, l_rev], one(32, T), t1[32:40, l_rev],
                                          t2[32:40, 0:1], ALU.mult, ALU.add))
                u = gsb[0:40, :]
                v.tensor_tensor(u, u, t2[:], ALU.subtract).then_inc(S["u_ready"], 1)
                dve.wait_ge(S["u_ready"], 1)
                link(v.memset(t1[:], 0.0))
                link(v.tensor_tensor_scan(t1[0:8, :], u[0:8, :], u[0:8, :], 0.0, ALU.max, ALU.max))
                link(v.tensor_tensor_scan(t1[32:40, c_rev], u[32:40, c_rev], u[32:40, c_rev], 0.0,
                                          ALU.max, ALU.max))
                link(v.tensor_tensor_scan(t1[32:40, l_rev], u[32:40, l_rev], u[32:40, l_rev],
                                          t1[32:40, 0:1], ALU.max, ALU.max))
                v.tensor_scalar(negm[:], t1[:, T:2 * T], -1.0, None, ALU.mult)
                v.tensor_tensor(t2[:, T:2 * T], t2[:, T:2 * T], t1[:, T:2 * T], ALU.add
                                ).then_inc(S["thr_in"], 1)

            dve.wait_ge(S["ld_bm"], 64)
            jobs = {J0: lambda: (gates(), dve.wait_ge(S["proj_free"], 5), conv_k(0))}
            for j in range(1, 4):
                jobs[J0 + j] = lambda j=j: conv_k(j)
            for j in range(4):
                jobs[J0 + 4 + j] = lambda j=j: (dve.wait_ge(S["proj_free"], 9), conv_grid(
                    QT[:, j, :], qraw[:, j, :], vec[:, V_CONV + 9 * j:V_CONV + 9 * (j + 1)], "qconv"))
            for m in range(MODB_EARLY):
                modb(m)
            for m in range(MODB_EARLY):
                modb_out(m)
            for m in range(MODB_EARLY, MODB_LATE):
                modb(m)
                if m > MODB_EARLY:
                    modb_out(m - 1)
                if m in jobs:
                    jobs[m]()
            modb_out(MODB_LATE - 1)
            scans()
            dve.wait_ge(S["uT_psum"], 1)
            v.tensor_copy(uT[:], ps[:, 0, 0:240].rearrange("p (b r) -> p b r", b=6)
                          ).then_inc(S["uT_ready"], 1)
            dve.wait_ge(S["uT_ready"], 1)

            def diagonals(h):
                dve.wait_ge(S["s_done"], h + 1)
                for d in range(2):
                    for b in range(2):
                        w = wexp[:, d, 2 + b, b * P:(b + 1) * P]
                        ins = v.scalar_tensor_tensor(
                            out=w, in0=ps[:, 2, d * T + b * P:d * T + (b + 1) * P],
                            scalar=uT[:, 2 + b, 32 * d + h:32 * d + h + 1],
                            in1=K[:, C_MASK + d * P:C_MASK + (d + 1) * P], op0=ALU.add, op1=ALU.add)
                    ins.then_inc(S["diag_in"], 1)

            def weigh(h):
                for d in range(2):
                    dve.wait_ge(S["exp_done"], 2 * h + d + 1)
                    w = flat2(wexp[:, d])
                    runs = [(0, 768), (896, 1024)] if d == 0 else [(0, 640), (768, 1024)]
                    parts = []
                    for a, z in runs:
                        parts += [(a, min(z, 512)), (512, z)] if a < 512 < z else [(a, z)]
                    for a, z in parts:
                        bank = a // 512
                        ins = v.scalar_tensor_tensor(
                            out=w[:, a:z], in0=ps[:, bank, a % 512:(z - 1) % 512 + 1],
                            scalar=DK ** -0.5, in1=w[:, a:z], op0=ALU.mult, op1=ALU.mult)
                    ins.then_inc(S["p_done"], 1)

            def flat2(ap):
                return ap.rearrange("p s j -> p (s j)")

            def divide(h):
                for d in range(2):
                    dve.wait_ge(S["num_done"], 4 * h + 2 * d + 2)
                    num = ps[:, 3 + d, :].rearrange("p (j n) -> p j n", j=2)
                    den = num[:, :, DV:DV + 1]
                    r = 32 * d + h
                    q = small[:, 4 + 2 * d:6 + 2 * d].unsqueeze(2)
                    link(v.tensor_copy(q, den))
                    link(v.scalar_tensor_tensor(out=q, in0=q, scalar=-1.0, in1=q,
                                                op0=ALU.mult, op1=ALU.max))
                    link(v.tensor_tensor(q, q, uT[:, 4:6, r:r + 1], ALU.max))
                    link(v.reciprocal(q, q))
                    for j in range(2):
                        o = hm[:, j, h * DV:(h + 1) * DV]
                        s = small[:, 4 + 2 * d + j:5 + 2 * d + j]
                        if d == 0:
                            ins = v.tensor_scalar(o, num[:, j, 0:DV], s, None, ALU.mult)
                        else:
                            ins = v.scalar_tensor_tensor(out=o, in0=num[:, j, 0:DV], scalar=s, in1=o,
                                                         op0=ALU.mult, op1=ALU.add)
                    ins.then_inc(S["num_free"], 1)
                    dve.wait_ge(S["num_free"], 2 * h + d + 1)

            for h in range(MH):
                diagonals(h)
                weigh(h)
                divide(h)

            for b in range(TB):
                sq = tmp[:, 4096 + b * FW:4096 + (b + 1) * FW]
                link(v.tensor_tensor(sq, hm[:, b, :], hm[:, b, :], ALU.mult))
                ins = v.reduce_sum(st[:, 16 + b * MH:16 + (b + 1) * MH],
                                   sq.rearrange("p (h d) -> p h d", h=MH), AX_X)
            ins.then_inc(S["hsq"], 1)
            dve.wait_ge(S["o_sig"], 1)
            dve.wait_ge(S["ld_gy"], 32)
            for b in range(TB):
                ins = v.tensor_tensor(A[:, b, FW:D], A[:, b, FW:D], gy[:, FW:D], ALU.mult)
            link(ins)
            dve.wait_ge(S["std"], 2)
            link(v.reciprocal(st[:, 40:56], st[:, 40:56]))
            for b in range(TB):
                for h in range(MH):
                    a = A[:, b, FW + h * DV:FW + (h + 1) * DV]
                    ins = v.scalar_tensor_tensor(out=a, in0=hm[:, b, h * DV:(h + 1) * DV],
                                                 scalar=st[:, 40 + b * MH + h:41 + b * MH + h], in1=a,
                                                 op0=ALU.mult, op1=ALU.mult)
            ins.then_inc(S["ym_ready"], 1)
            dve.wait_ge(S["std"], 3)
            link(v.reciprocal(st[:, 32:40], st[:, 32:40]))
            for b in range(TB):
                for g in range(FG):
                    a = A[:, b, g * GW:(g + 1) * GW]
                    ins = v.scalar_tensor_tensor(
                        out=a, in0=a, scalar=st[:, 32 + b * FG + g:33 + b * FG + g],
                        in1=gy[:, g * GW:(g + 1) * GW], op0=ALU.mult, op1=ALU.mult)
            ins.then_inc(S["y_ready"], 1)
            v.memset(small[:, 1:2], 0.0).then_inc(S["out_free"], 4)

            dve.wait_ge(S["ld_gffn"], 16)
            dve.wait_ge(S["ld_sc2"], 16)
            v.scalar_tensor_tensor(out=g2, in0=ga2, scalar=1.0, in1=g2, op0=ALU.add, op1=ALU.mult
                                   ).then_inc(S["g2_ready"], 1)

            dve.wait_ge(S["ld_x2"], 16)
            dve.wait_ge(S["ld_ga1"], 16)
            for n in range(4):
                modb(MODB_LATE + n)
                if n >= 1:
                    modb_out(MODB_LATE + n - 1)
                dve.wait_ge(S["w_free"], 32 + 2 * n + 2)
                for b in range(TB):
                    o = B[:, b, n * CH:(n + 1) * CH]
                    t = xtmp[:, b * CH:(b + 1) * CH]
                    v.tensor_tensor(t, ps[:, 2 * (n % 2) + b, :], ga1[:, n * CH:(n + 1) * CH],
                                    ALU.mult).then_inc(S["out_free"], 1)
                    dve.wait_ge(S["out_free"], 4 + 2 * n + b + 1)
                    v.tensor_tensor(o, o, t, ALU.add).then_inc(S["x1_ready"], 1)
            modb_out(MODB - 1)

            dve.wait_ge(S["g2_ready"], 1)
            dve.wait_ge(S["ld_sh2"], 16)
            dve.wait_ge(S["std2"], 1)
            link(v.reciprocal(st[:, 4:6], st[:, 2:4]))
            for part in (slice(0, FW), slice(FW, D)):
                for b in range(TB):
                    link(v.scalar_tensor_tensor(out=A[:, b, part], in0=B[:, b, part],
                                                scalar=st[:, 4 + b:5 + b], in1=g2[:, part],
                                                op0=ALU.mult, op1=ALU.mult))
                    v.tensor_tensor(A[:, b, part], A[:, b, part], sh2[:, part], ALU.add
                                    ).then_inc(S["h2_ready"], 1)

            v.memset(small[:, 3:4], 0.0).then_inc(S["u_free"], 4)
            v.memset(small[:, 4:5], 0.0).then_inc(S["tail_free"], 1)
            iota = K[:, C_IOTA:C_IOTA + TOPK]
            steps = dve_chain(dve)

            def pick(g, n):
                step = steps(n)

                def top16(values, indices, src, scratch):
                    dve.nop(nofuse=True)
                    step(v.max(values[:, 0:8], src))
                    dve.nop(nofuse=True)
                    v.max_index(indices[:, 0:8], values[:, 0:8], src)
                    step(v.match_replace(scratch, values[:, 0:8], src, LOWEST))
                    dve.nop(nofuse=True)
                    step(v.max(values[:, 8:16], scratch))
                    dve.nop(nofuse=True)
                    return v.max_index(indices[:, 8:16], values[:, 8:16], scratch)

                grid = [P, TOPK, TOPK]
                sq = lambda t: t.rearrange("p (a c) -> p a c", a=TOPK)
                step(v.tensor_copy(stage, sc[:, bass.ds(g * (2 * NK), 2 * NK)]))
                for p_ in range(2):
                    ins = top16(sv[:, 16 * p_:16 * p_ + 16], siu[:, 16 * p_:16 * p_ + 16],
                                stage[:, p_ * NK:(p_ + 1) * NK], work[:, p_ * NK:(p_ + 1) * NK])
                step(ins)
                v.tensor_copy(si, siu)
                step(v.tensor_tensor(sq(cand), sv[:, 0:16].unsqueeze(2).to_broadcast(grid),
                                     sv[:, 16:32].unsqueeze(1).to_broadcast(grid), ALU.add))
                step(top16(top, pos, cand, work))
                for p_ in range(2):
                    op, k = (ALU.logical_shift_right, 4) if p_ == 0 else (ALU.bitwise_and, 15)
                    step(v.tensor_scalar(half, pos, k, None, op))
                    step(v.tensor_copy(halff, half))
                    step(v.tensor_tensor(sq(work), halff.unsqueeze(2).to_broadcast(grid),
                                         iota.unsqueeze(1).to_broadcast(grid), ALU.is_equal))
                    step(v.tensor_tensor(sq(work), sq(work), si[:, 16 * p_:16 * p_ + 16].unsqueeze(1)
                                         .to_broadcast(grid), ALU.mult))
                    step(v.reduce_sum(sel[:, p_ * 16:(p_ + 1) * 16], sq(work), AX_X))
                step(v.scalar_tensor_tensor(out=eflt, in0=sel[:, 0:16], scalar=float(NK),
                                            in1=sel[:, 16:32], op0=ALU.mult, op1=ALU.add))
                v.tensor_tensor(topd[:, bass.ds(g * TOPK, TOPK)], top,
                                top[:, 0:1].to_broadcast([P, TOPK]), ALU.subtract)
                v.tensor_copy(eidx[:, bass.ds(g * TOPK, TOPK)], eflt).then_inc(S["picked"], 1)
                dve.wait_ge(S["picked"], n + 1)

            def weights(g, nth):
                dve.wait_ge(S["gelu_done"], nth)
                v.reciprocal(small[:, 1:2], sums[:, bass.ds(g, 1)]).then_inc(S["sums_inv"], 1)
                dve.wait_ge(S["sums_inv"], nth)
                v.scalar_tensor_tensor(
                    out=wgt[:, bass.ds(g * TOPK, TOPK)], in0=act_t[:, bass.ds(g * TOPK, TOPK)],
                    scalar=small[:, 1:2], in1=soft[:, bass.ds(g * TOPK, TOPK)],
                    op0=ALU.mult, op1=ALU.mult).then_inc(S["wgt_ready"], 1)

            def dot(g, b, first=False):
                for r in range(TOPK):
                    s = r % 4
                    if r == TOPK // 2 and not first:
                        weights(g - 1, g)
                    if r == 8 and first:
                        dve.wait_ge(S["score_ready"], 3)
                        pick(2, 2)
                    dve.wait_ge(u_ld[s], g * 64 + 16 * (r // 4 + 1))
                    v.scalar_tensor_tensor(
                        out=ring[:, 4 + s, :], in0=ring[:, 4 + s, :], scalar=1.0, in1=A[:, b, :],
                        op0=ALU.mult, op1=ALU.mult,
                        accum_out=dots[:, bass.ds(g * TOPK + r, 1)]).then_inc(S["u_free"], 1)
                dve.wait_ge(S["u_free"], g * TOPK + (TOPK + 4))
                v.memset(small[:, 2:3], 0.0).then_inc(S["dots_ready"], 1)

            dve.wait_ge(S["score_ready"], 1)
            pick(0, 0)
            pick(1, 1)
            dot(0, 0, first=True)
            dot(1, 0)
            pick(3, 3)
            dve.wait_ge(S["score_ready"], 8)
            for b, g0, g1 in ((0, 2, PH), (1, PH, 2 * PH - 2)):
                with dve.Fori(g0, g1) as g:
                    dot(g, b)
                    pick(g + 2, g + 2)
            with dve.Fori(2 * PH - 2, 2 * PH) as g:
                dot(g, 1)

            share = A[:, 1, :]

            def tail(i):
                dve.wait_ge(v_ld[TAIL_SLOT], 16 * (TAIL_RANK // 4 + i + 1))
                rows_v = ring[:, TAIL_SLOT, :]
                rank = TAIL_RANK + 4 * i + TAIL_SLOT
                w = wgt[:, rank:rank + 1]
                if i == 0:
                    v.tensor_scalar(share, rows_v, w, None, ALU.mult).then_inc(S["tail_free"], 1)
                else:
                    dve.wait_ge(S["tail_free"], i + 1)
                    v.scalar_tensor_tensor(out=share, in0=rows_v, scalar=w, in1=share,
                                           op0=ALU.mult, op1=ALU.add).then_inc(S["tail_free"], 1)

            def add_peer(b):
                for half_ in range(2):
                    for n in (2 * half_, 2 * half_ + 1):
                        t = ring[:, 4 + b, n * CH:(n + 1) * CH]
                        ins = v.tensor_tensor(t, ps[:, 4 * b + n, :], ga2[:, n * CH:(n + 1) * CH],
                                              ALU.mult)
                    link(ins)
                    part = slice(half_ * FW, (half_ + 1) * FW)
                    v.tensor_tensor(B[:, b, part], B[:, b, part], ring[:, 4 + b, part], ALU.add
                                    ).then_inc(S["ssq3"], 1)

            def final_norm(b):
                dve.wait_ge(S["std3"], b + 1)
                link(v.reciprocal(st[:, 4 + b:5 + b], st[:, 2 + b:3 + b]))
                for half_ in range(2):
                    part = slice(half_ * FW, (half_ + 1) * FW)
                    v.scalar_tensor_tensor(out=B[:, b, part], in0=B[:, b, part],
                                           scalar=st[:, 4 + b:5 + b], in1=gy[:, part],
                                           op0=ALU.mult, op1=ALU.mult
                                           ).then_inc(S["final_ready"], 1)

            before = TAIL_QUADS - TOPK // 4
            dve.wait_ge(S["wgt_ready"], TB * PH - 1)
            for i in range(before):
                tail(i)
                if i == 0:
                    dve.wait_ge(S["pair_free"], 4 + P)
                    dve.wait_ge(S["ld_ga2"], 16)
                    add_peer(0)
            weights(2 * PH - 1, 2 * PH)
            dve.wait_ge(S["wgt_ready"], TB * PH)
            for i in range(before, TAIL_QUADS):
                tail(i)
            dve.wait_ge(S["tail_free"], TAIL_QUADS + 1)
            link(v.tensor_tensor(share, share, ga2[:], ALU.mult))
            link(v.tensor_tensor(B[:, 1, :], B[:, 1, :], share, ALU.add))
            dve.wait_ge(S["ld_gfin"], 16)
            final_norm(0)
            dve.wait_ge(S["pair_free"], 4 + TAIL_RANK + 3 * TAIL_QUADS)
            add_peer(1)
            final_norm(1)


INPUTS = ["x", "c", "ctx", "c_ctx", "w_mod", "b_mod", "g_norm_mix", "g_norm_ffn", "w_in", "b_gate",
          "conv_qk", "g_fourier", "g_mlstm", "w_out", "w_query", "sub_keys", "expert_u", "expert_v",
          "g_final"]


def kernel(**inputs):
    from concourse import bacc
    from concourse.bass_utils import run_bass_kernel_spmd

    nc = bacc.Bacc("TRN2", target_bir_lowering=False, num_devices=1)
    arrays = {f"in_{n}": np.ascontiguousarray(inputs[n]) for n in INPUTS}
    arrays["in_consts"] = constants()
    args = [nc.dram_tensor(n, a.shape, mybir.dt.from_np(a.dtype), kind="ExternalInput").ap()
            for n, a in arrays.items()]
    out = nc.dram_tensor("out_x", (1, T, D), F32, kind="ExternalOutput").ap()
    build(nc, *args, out)
    result = run_bass_kernel_spmd(nc, [arrays], core_ids=[0])
    return result.results[0]["out_x"]
```
